# Optimizing a Trainium2 kernel written in Bass

```python
import math
import jax, jax.numpy as jnp
from jax import lax
import numpy as np

D_MODEL = 1024
BATCH = 1
SEQ = 512
DEPTH = 2

CHUNK = 64
HEAD_DIM = 64
CONV_WIDTH = 4
ROPE_THETA = 10000.0
EPS = 1e-6
N_BRANCH = 4

LRU_WIDTH = D_MODEL
LRU_BLOCKS = D_MODEL // HEAD_DIM
LRU_BLOCK = LRU_WIDTH // LRU_BLOCKS
LRU_C = 8.0
SSD_WIDTH = D_MODEL
SSD_HEAD_DIM = 64
SSD_HEADS = SSD_WIDTH // SSD_HEAD_DIM
SSD_GROUPS = 2
SSD_STATE = 128
SSD_CONV_CH = SSD_WIDTH + 2 * SSD_GROUPS * SSD_STATE
SWA_HEADS = D_MODEL // HEAD_DIM
SWA_KV_HEADS = 4
SWA_WIDTH = SWA_HEADS * HEAD_DIM
SWA_KV_WIDTH = SWA_KV_HEADS * HEAD_DIM
WINDOW = 128
WINDOW_CHUNKS = WINDOW // CHUNK
DIFF_HEADS = D_MODEL // (2 * HEAD_DIM)
DIFF_WIDTH = DIFF_HEADS * 2 * HEAD_DIM
Q_BLOCK = 128

IN_SIZES = (LRU_WIDTH, LRU_WIDTH,
            SSD_WIDTH, SSD_CONV_CH, SSD_HEADS,
            SWA_WIDTH, SWA_KV_WIDTH, SWA_KV_WIDTH, SWA_WIDTH,
            DIFF_WIDTH, DIFF_WIDTH, DIFF_WIDTH, DIFF_WIDTH,
            N_BRANCH * D_MODEL)
D_IN = sum(IN_SIZES)

kernel_name = "hybrid_gated_parallel_mixers"

def _split_columns(t, sizes):
    out, off = [], 0
    for s in sizes:
        out.append(t[..., off:off + s])
        off += s
    return out

def _rms_norm(x, g):
    xf = x.astype(jnp.float32)
    y = xf * lax.rsqrt(jnp.mean(xf * xf, axis=-1, keepdims=True) + EPS)
    return (y * g.astype(jnp.float32)).astype(x.dtype)

def _causal_conv(x, w, b):
    c = x.shape[-1]
    y = lax.conv_general_dilated(x, w[:, None, :].astype(x.dtype), window_strides=(1,),
                                 padding=[(CONV_WIDTH - 1, 0)],
                                 dimension_numbers=('NWC', 'WIO', 'NWC'),
                                 feature_group_count=c)
    return y + b.astype(x.dtype)

def _rope_tables(seq, dim):
    inv = 1.0 / (ROPE_THETA ** (jnp.arange(0, dim, 2, dtype=jnp.float32) / dim))
    ang = jnp.arange(seq, dtype=jnp.float32)[:, None] * inv[None, :]
    return jnp.cos(ang), jnp.sin(ang)

def _apply_rope(x, cos, sin):
    half = x.shape[-1] // 2
    shp = (1, x.shape[1]) + (1,) * (x.ndim - 3) + (half,)
    c, s = cos.reshape(shp), sin.reshape(shp)
    xf = x.astype(jnp.float32)
    x1, x2 = xf[..., :half], xf[..., half:]
    return jnp.concatenate([x1 * c - x2 * s, x2 * c + x1 * s], axis=-1).astype(x.dtype)

def _combine(e1, e2):
    a1, b1 = e1
    a2, b2 = e2
    return a1 * a2, a2 * b1 + b2

def _rglru_branch(xa, ga, conv_w, conv_b, w_r, b_r, w_i, b_i, lam):
    f32 = jnp.float32
    bsz, s, w = xa.shape
    u = _causal_conv(xa, conv_w, conv_b)
    ub = u.reshape(bsz, s, LRU_BLOCKS, LRU_BLOCK)
    r = jax.nn.sigmoid(jnp.einsum('bshi,hij->bshj', ub, w_r).reshape(bsz, s, w) + b_r)
    i = jax.nn.sigmoid(jnp.einsum('bshi,hij->bshj', ub, w_i).reshape(bsz, s, w) + b_i)
    log_a = -LRU_C * r.astype(f32) * jax.nn.softplus(-lam.astype(f32))
    a = jnp.exp(log_a)
    beta = jnp.sqrt(-jnp.expm1(2.0 * log_a))
    _, h = lax.associative_scan(_combine, (a, beta * (i * u).astype(f32)), axis=1)
    return h.astype(xa.dtype) * jax.nn.silu(ga)

def _ssd_branch(z, xbc, dt_raw, conv_w, conv_b, dt_bias, a_log, d_skip, norm_g):
    f32 = jnp.float32
    bsz, s, _ = z.shape
    nc = s // CHUNK
    hg = SSD_HEADS // SSD_GROUPS
    gn = SSD_GROUPS * SSD_STATE
    xbc = jax.nn.silu(_causal_conv(xbc, conv_w, conv_b))
    xs = xbc[..., :SSD_WIDTH].reshape(bsz, nc, CHUNK, SSD_GROUPS, hg, SSD_HEAD_DIM).astype(f32)
    bm = xbc[..., SSD_WIDTH:SSD_WIDTH + gn].reshape(bsz, nc, CHUNK, SSD_GROUPS, SSD_STATE).astype(f32)
    cm = xbc[..., SSD_WIDTH + gn:].reshape(bsz, nc, CHUNK, SSD_GROUPS, SSD_STATE).astype(f32)
    dt = jax.nn.softplus(dt_raw.astype(f32) + dt_bias.astype(f32)).reshape(bsz, nc, CHUNK, SSD_GROUPS, hg)
    a = -jnp.exp(a_log.astype(f32)).reshape(SSD_GROUPS, hg)
    cs = jnp.cumsum(dt * a, axis=2)
    xdt = xs * dt[..., None]
    cs_t = jnp.moveaxis(cs, 2, -1)
    seg = cs_t[..., :, None] - cs_t[..., None, :]
    causal = jnp.tril(jnp.ones((CHUNK, CHUNK), dtype=bool))
    decay = jnp.exp(jnp.where(causal, seg, -jnp.inf))
    cb = jnp.einsum('bclgn,bcsgn->bcgls', cm, bm)
    y_intra = jnp.einsum('bcgjls,bcsgjp->bclgjp', cb[:, :, :, None] * decay, xdt)
    decay_end = jnp.exp(cs[:, :, -1:] - cs)
    states = jnp.einsum('bclgn,bclgj,bclgjp->bcgjpn', bm, decay_end, xdt)
    chunk_decay = jnp.exp(cs[:, :, -1])[..., None, None]
    _, acc = lax.associative_scan(_combine, (chunk_decay, states), axis=1)
    prev = jnp.concatenate([jnp.zeros_like(acc[:, :1]), acc[:, :-1]], axis=1)
    y_inter = jnp.einsum('bclgn,bcgjpn,bclgj->bclgjp', cm, prev, jnp.exp(cs))
    y = y_intra + y_inter + d_skip.astype(f32).reshape(SSD_GROUPS, hg)[..., None] * xs
    y = y.reshape(bsz, s, SSD_WIDTH)
    yg = (y * jax.nn.silu(z.astype(f32))).reshape(bsz, s, SSD_GROUPS, SSD_WIDTH // SSD_GROUPS)
    yg = yg * lax.rsqrt(jnp.mean(yg * yg, axis=-1, keepdims=True) + EPS)
    return (yg.reshape(bsz, s, SSD_WIDTH) * norm_g.astype(f32)).astype(z.dtype)

def _shift_chunks(t, j):
    if j == 0:
        return t
    pad = [(0, 0)] * t.ndim
    pad[1] = (j, 0)
    return jnp.pad(t, pad)[:, :t.shape[1]]

def _swa_branch(q, k, v, g, sinks, cos, sin):
    f32 = jnp.float32
    bsz, s, _ = q.shape
    nc = s // CHUNK
    rep = SWA_HEADS // SWA_KV_HEADS
    q = _apply_rope(q.reshape(bsz, s, SWA_HEADS, HEAD_DIM), cos, sin)
    k = _apply_rope(k.reshape(bsz, s, SWA_KV_HEADS, HEAD_DIM), cos, sin)
    v = v.reshape(bsz, s, SWA_KV_HEADS, HEAD_DIM)
    qc = q.reshape(bsz, nc, CHUNK, SWA_KV_HEADS, rep, HEAD_DIM)
    kc = k.reshape(bsz, nc, CHUNK, SWA_KV_HEADS, HEAD_DIM)
    vc = v.reshape(bsz, nc, CHUNK, SWA_KV_HEADS, HEAD_DIM)
    offs = range(WINDOW_CHUNKS - 1, -1, -1)
    kw = jnp.concatenate([_shift_chunks(kc, j) for j in offs], axis=2)
    vw = jnp.concatenate([_shift_chunks(vc, j) for j in offs], axis=2)
    slot = jnp.arange(WINDOW_CHUNKS * CHUNK)[None, :] // CHUNK
    valid = jnp.arange(nc)[:, None] - (WINDOW_CHUNKS - 1 - slot) >= 0
    sc = jnp.einsum('bclkrd,bcmkd->bckrlm', qc, kw, preferred_element_type=f32) * (HEAD_DIM ** -0.5)
    sc = jnp.where(valid[None, :, None, None, None, :], sc, -jnp.inf)
    sink = sinks.astype(f32).reshape(SWA_KV_HEADS, rep)[None, None, :, :, None, None]
    m = jnp.maximum(jnp.max(sc, axis=-1, keepdims=True), sink)
    p = jnp.exp(sc - m)
    p = p / (jnp.sum(p, axis=-1, keepdims=True) + jnp.exp(sink - m))
    o = jnp.einsum('bckrlm,bcmkd->bclkrd', p.astype(vw.dtype), vw).reshape(bsz, s, SWA_WIDTH)
    return o * jax.nn.silu(g)

def _diff_branch(q, k, v, g, lq1, lk1, lq2, lk2, norm_g, lam_init, cos, sin):
    f32 = jnp.float32
    bsz, s, _ = q.shape
    nb = s // Q_BLOCK
    q = _apply_rope(q.reshape(bsz, s, DIFF_HEADS, 2, HEAD_DIM), cos, sin)
    k = _apply_rope(k.reshape(bsz, s, DIFF_HEADS, 2, HEAD_DIM), cos, sin)
    v = v.reshape(bsz, s, DIFF_HEADS, 2 * HEAD_DIM)
    lam = (jnp.exp(jnp.sum(lq1.astype(f32) * lk1.astype(f32)))
           - jnp.exp(jnp.sum(lq2.astype(f32) * lk2.astype(f32))) + lam_init)
    qb = jnp.moveaxis(q.reshape(bsz, nb, Q_BLOCK, DIFF_HEADS, 2, HEAD_DIM), 1, 0)
    key_chunk = jnp.arange(s) // CHUNK

    def block(args):
        qi, bi = args
        q_chunk = (bi * Q_BLOCK + jnp.arange(Q_BLOCK)) // CHUNK
        mask = key_chunk[None, :] <= q_chunk[:, None]
        sc = jnp.einsum('bqhtd,bkhtd->bhtqk', qi, k, preferred_element_type=f32) * (HEAD_DIM ** -0.5)
        p = jax.nn.softmax(jnp.where(mask, sc, -jnp.inf), axis=-1)
        attn = p[:, :, 0] - lam * p[:, :, 1]
        return jnp.einsum('bhqk,bkhe->bqhe', attn.astype(v.dtype), v)

    o = lax.map(block, (qb, jnp.arange(nb)))
    o = jnp.moveaxis(o, 0, 1).reshape(bsz, s, DIFF_HEADS, 2 * HEAD_DIM)
    o = _rms_norm(o, norm_g) * (1.0 - lam_init)
    return o.reshape(bsz, s, DIFF_WIDTH) * jax.nn.silu(g)

def setup_inputs(seed: int = 0) -> dict:
    key = jax.random.key(seed)
    ks = jax.random.split(key, 32)
    L, D = DEPTH, D_MODEL
    nrm = jax.random.normal
    a0 = jax.random.uniform(ks[9], (L, LRU_WIDTH), minval=0.9, maxval=0.999)
    dt0 = jnp.exp(jax.random.uniform(ks[13], (L, SSD_HEADS), minval=math.log(1e-3), maxval=math.log(1e-1)))
    return {
        "x": nrm(ks[0], (BATCH, SEQ, D), jnp.float32),
        "pre_norm_g": 1.0 + 0.05 * nrm(ks[1], (L, D)),
        "w_in": nrm(ks[2], (L, D, D_IN)) * D ** -0.5,
        "b_merge": 0.1 * nrm(ks[3], (L, N_BRANCH * D)),
        "lru_conv_w": nrm(ks[4], (L, CONV_WIDTH, LRU_WIDTH)) * CONV_WIDTH ** -0.5,
        "lru_conv_b": 0.01 * nrm(ks[5], (L, LRU_WIDTH)),
        "lru_w_r": nrm(ks[6], (L, LRU_BLOCKS, LRU_BLOCK, LRU_BLOCK)) * LRU_BLOCK ** -0.5,
        "lru_b_r": 0.01 * nrm(ks[7], (L, LRU_WIDTH)),
        "lru_w_i": nrm(ks[8], (L, LRU_BLOCKS, LRU_BLOCK, LRU_BLOCK)) * LRU_BLOCK ** -0.5,
        "lru_b_i": 0.01 * nrm(ks[10], (L, LRU_WIDTH)),
        "lru_lambda": jnp.log(a0) - jnp.log1p(-a0),
        "ssd_conv_w": nrm(ks[11], (L, CONV_WIDTH, SSD_CONV_CH)) * CONV_WIDTH ** -0.5,
        "ssd_conv_b": 0.01 * nrm(ks[12], (L, SSD_CONV_CH)),
        "ssd_dt_bias": dt0 + jnp.log(-jnp.expm1(-dt0)),
        "ssd_a_log": jnp.log(jax.random.uniform(ks[14], (L, SSD_HEADS), minval=1.0, maxval=16.0)),
        "ssd_d": 1.0 + 0.1 * nrm(ks[15], (L, SSD_HEADS)),
        "ssd_norm_g": 1.0 + 0.05 * nrm(ks[16], (L, SSD_WIDTH)),
        "swa_sinks": 0.5 * nrm(ks[17], (L, SWA_HEADS)),
        "diff_lq1": 0.1 * nrm(ks[18], (L, HEAD_DIM)),
        "diff_lk1": 0.1 * nrm(ks[19], (L, HEAD_DIM)),
        "diff_lq2": 0.1 * nrm(ks[20], (L, HEAD_DIM)),
        "diff_lk2": 0.1 * nrm(ks[21], (L, HEAD_DIM)),
        "diff_norm_g": 1.0 + 0.05 * nrm(ks[22], (L, 2 * HEAD_DIM)),
        "w_branch": nrm(ks[23], (L, N_BRANCH, D, D)) * D ** -0.5,
        "w_out": nrm(ks[24], (L, D, D)) * D ** -0.5,
        "post_norm_g": 1.0 + 0.05 * nrm(ks[25], (L, D)),
    }

def reference(x, pre_norm_g, w_in, b_merge, lru_conv_w, lru_conv_b, lru_w_r, lru_b_r,
              lru_w_i, lru_b_i, lru_lambda, ssd_conv_w, ssd_conv_b, ssd_dt_bias, ssd_a_log,
              ssd_d, ssd_norm_g, swa_sinks, diff_lq1, diff_lk1, diff_lq2, diff_lk2,
              diff_norm_g, w_branch, w_out, post_norm_g):
    bsz, s, d = x.shape
    cos, sin = _rope_tables(s, HEAD_DIM)
    for l in range(DEPTH):
        lam_init = 0.8 - 0.6 * math.exp(-0.3 * l)
        h = _rms_norm(x, pre_norm_g[l])
        proj = jnp.einsum('bsd,de->bse', h, w_in[l])
        (xa, ga, z, xbc, dt_raw, qc, kc, vc, gc,
         qd, kd, vd, gd, merge) = _split_columns(proj, IN_SIZES)
        ya = _rglru_branch(xa, ga, lru_conv_w[l], lru_conv_b[l], lru_w_r[l], lru_b_r[l],
                           lru_w_i[l], lru_b_i[l], lru_lambda[l])
        yb = _ssd_branch(z, xbc, dt_raw, ssd_conv_w[l], ssd_conv_b[l], ssd_dt_bias[l],
                         ssd_a_log[l], ssd_d[l], ssd_norm_g[l])
        yc = _swa_branch(qc, kc, vc, gc, swa_sinks[l], cos, sin)
        yd = _diff_branch(qd, kd, vd, gd, diff_lq1[l], diff_lk1[l], diff_lq2[l], diff_lk2[l],
                          diff_norm_g[l], lam_init, cos, sin)
        ys = jnp.stack([ya, yb, yc, yd], axis=2)
        yproj = jnp.einsum('bsnw,nwd->bsnd', ys, w_branch[l])
        gates = jax.nn.sigmoid((merge + b_merge[l]).astype(jnp.float32)).astype(x.dtype)
        merged = jnp.sum(gates.reshape(bsz, s, N_BRANCH, d) * yproj, axis=2)
        out = jnp.einsum('bsd,de->bse', merged, w_out[l])
        x = x + _rms_norm(out, post_norm_g[l])
    return x


_drawn_inputs = setup_inputs


def setup_inputs(seed=0):
    import zlib

    import numpy as np

    out = dict(_drawn_inputs(seed))
    spreads = {}
    factors = {'lru_conv_b': 4.63,
     'lru_b_r': 64.0,
     'lru_b_i': 64.0,
     'ssd_conv_b': 4.549,
     'swa_sinks': 39.128,
     'diff_lk1': 8.0,
     'diff_lq2': 3.87,
     'diff_norm_g': 3.1}
    for name, (base, spread) in spreads.items():
        noise = np.random.default_rng([zlib.crc32(name.encode()), seed]).standard_normal(out[name].shape)
        drawn = base * np.exp(spread * noise) if base else spread * noise
        out[name] = __import__('jax').numpy.asarray(drawn.astype(out[name].dtype))
    for name, factor in factors.items():
        out[name] = (out[name] * factor).astype(out[name].dtype)
    return out
```

```python
import math
from contextlib import ExitStack

import numpy as np

import concourse.bass as bass
from concourse import mybir

F32 = mybir.dt.float32
F16 = mybir.dt.float16
ACT = mybir.ActivationFunctionType
ALU = mybir.AluOpType
AX = mybir.AxisListType.X

P = 128
D = 1024
S = 512
L = 2
KT = D // P
ST = S // P
HD = 64
PW = 256
EPS = 1e-6
WS = 64.0
IWS = 1.0 / WS
NS = 2
NB = 2
NEG = -1e30

C_XA, C_GA, C_Z, C_XBC = 0, D, 2 * D, 3 * D
C_DT = C_XBC + D + 512
C_QC = C_DT + 16
C_KC, C_VC, C_GC = C_QC + D, C_QC + D + 256, C_QC + D + 512
C_QD = C_GC + D
C_KD, C_VD, C_GD, C_MG = C_QD + D, C_QD + 2 * D, C_QD + 3 * D, C_QD + 4 * D

PANELS = []
for _j in range(4):
    PANELS += [("xa", _j, "in", C_XA + PW * _j), ("ga", _j, "in", C_GA + PW * _j)]
PANELS += [("conv", 8, "in", C_XBC + D), ("conv", 10, "in", C_XBC + D + PW),
           ("kc", 0, "in", C_KC), ("vc", 0, "in", C_VC)]
for _g in range(2):
    PANELS += [("conv", 4 * _g, "in", C_XBC + 2 * _g * PW), ("conv", 4 * _g + 2, "in", C_XBC + (2 * _g + 1) * PW),
               ("z", 2 * _g, "in", C_Z + 2 * _g * PW), ("z", 2 * _g + 1, "in", C_Z + (2 * _g + 1) * PW)]


def _merge(n):
    out = []
    for c in range(4):
        out += [("mg", 4 * n + c, "in", C_MG + n * D + PW * c), ("br", 4 * n + c, "br", PW * c)]
    return out


PANELS += _merge(0)
for _j in range(4):
    PANELS += [("qc", _j, "in", C_QC + PW * _j), ("gc", _j, "in", C_GC + PW * _j)]
PANELS += _merge(1)
for _j in range(4):
    PANELS += [("qd", _j, "in", C_QD + PW * _j), ("kd", _j, "in", C_KD + PW * _j),
               ("vd", _j, "in", C_VD + PW * _j), ("gd", _j, "in", C_GD + PW * _j)]
PANELS += _merge(2) + _merge(3)
PANELS += [("out", c, "out", PW * c) for c in range(4)]
NP = len(PANELS)
SLOT = {(k, i): p for p, (k, i, _, _) in enumerate(PANELS)}

VECTOR_FREES = {"ga", "z", "gc", "gd", "br"}
ROPES = ["kc"] + ["qc"] * 4 + ["qd", "kd"] * 4
SSD_SLOT = [16, 17, 18, 19, 21, 22, 23, 24]
SSD_END = {20: 0, 25: 1}
SWA0 = SLOT[("qc", 0)] + 2
DIFF0 = SLOT[("qd", 0)] + 4
DIFF_END = {DIFF0 + 4 * h + 4: h for h in range(4)}
CONV_SLOTS = [p for p in range(NP) if PANELS[p][0] in ("xa", "conv")]


def freed_by_vector(tile):
    return PANELS[tile // 2][0] in VECTOR_FREES


def act_frees(tile):
    return sum(not freed_by_vector(t) for t in range(tile + 1))


def dve_frees(tile):
    return sum(freed_by_vector(t) for t in range(tile + 1))


def gate_writes(tile):
    return sum(PANELS[t // 2][0] in ("ga", "z", "gc", "gd", "mg") for t in range(tile))


def gate_uses(tile):
    return sum(PANELS[t // 2][0] in ("ga", "z", "gc", "gd") for t in range(tile + 1))


def conv_tiles(p):
    return 2 * sum(q < p for q in CONV_SLOTS)


K_ID, K_TRI, K_STRICT, K_ONES, K_COS, K_SIN, K_ML, K_MR = 0, 128, 256, 384, 512, 1024, 1536, 1664
K_N = 1920
A_G, A_BM, A_CW, A_CB, A_BR, A_BI, A_LAM, A_N = 0, 8, 40, 72, 80, 88, 96, 104
B_CW, B_CB, B_NG, B_DG, B_N = 0, 48, 60, 68, 69
R_DTB, R_AL, R_D, R_SINK, R_LQ, R_LI, R_N = 0, 16, 32, 48, 64, 320, 322


def program(nc, x, w_in, w_branch, w_out, w_r, w_i, cols_a, cols_b, rows, post_g, consts, out):
    ctx = ExitStack()
    with ctx:
        def sb(name, shape, dt=F32):
            return ctx.enter_context(nc.sbuf_tensor(name, shape, dt))

        xres = sb("xres", [P, ST, D])
        hT = sb("hT", [P, 2, KT, S], F16)
        M = sb("M", [P, 8, S])
        ys = sb("ys", [P, 2, 4096])
        X = sb("X", [P, 11264])
        Y = sb("Y", [P, 8448])
        stage = sb("stage", [P, NS, KT, PW])
        wsp = sb("wsp", [P, NB, 2, KT, PW], F16)
        G = sb("G", [P, 2, S])
        T = sb("T", [P, 1032])
        K = sb("K", [P, K_N])
        rowp = sb("rowp", [P, R_N])
        colA = sb("colA", [P, A_N])
        halfA = sb("halfA", [P, A_N])
        colB = sb("colB", [P, B_N])
        small = sb("small", [P, 160])
        PS = ctx.enter_context(nc.psum_tensor("PS", [P, 8, 512], F32))

        ident, tri, strict, ones = (K[:, a:a + P] for a in (K_ID, K_TRI, K_STRICT, K_ONES))
        cosT, sinT = K[:, K_COS:K_COS + S], K[:, K_SIN:K_SIN + S]

        def half(b, part):
            return ys[:, b, 2048 * part:2048 * part + 2048].bitcast(F16).rearrange("p (t s) -> p t s", s=S)

        Y_HI = [half(0, 0), half(1, 0)]
        Y_LO = [half(0, 1), half(1, 1)]

        xpad = T[:, 0:1032].rearrange("p (u s) -> p u s", u=2)
        cbuf, rbuf, wbuf, abuf = (M[:, 2 * i:2 * i + 2, :] for i in range(4))
        lru_mem = ys[:, 1, :].rearrange("p (t s) -> p t s", s=S)
        vbuf, gbuf, hbuf = (lru_mem[:, 2 * i:2 * i + 2, :] for i in range(3))
        BT = X[:, 0:1024].rearrange("p (g s) -> p g s", g=2)
        CT = X[:, 1024:2048].rearrange("p (g s) -> p g s", g=2)
        Bseq = X[:, 2048:3072].rearrange("p (c n) -> p c n", c=ST)
        xs = [X[:, 3072 + 4096 * g:5120 + 4096 * g].rearrange("p (c n) -> p c n", c=ST) for g in range(2)]
        z = [X[:, 5120 + 4096 * g:7168 + 4096 * g].rearrange("p (c n) -> p c n", c=ST) for g in range(2)]
        sE = X[:, 0:2048].rearrange("p (e k n) -> p e k n", e=2, k=4)
        sPT = X[:, 2048:4096].rearrange("p (e k n) -> p e k n", e=2, k=4)
        sy = X[:, 4096:4608].rearrange("p (e u n) -> p e u n", e=2, u=2)
        def pair(at):
            return [X[:, at + 1024 * b:at + 1024 * b + 1024].rearrange("p (u s) -> p u s", u=2) for b in range(2)]
        qD, kD, gD = pair(0), pair(2048), pair(4096)
        vD = [X[:, 6144 + 1024 * b:7168 + 1024 * b].rearrange("p (c n) -> p c n", c=ST) for b in range(2)]
        rraw, rswap, rcos = (X[:, 8192 + 1024 * b:9216 + 1024 * b].rearrange("p (u s) -> p u s", u=2) for b in range(3))
        kC = Y[:, 0:1024].rearrange("p (u s) -> p u s", u=2)
        kCs = Y[:, 1024:2048].rearrange("p (u s) -> p u s", u=2)
        vC = Y[:, 2048:3072].rearrange("p (c n) -> p c n", c=ST)
        qC = [Y[:, 3072 + 1024 * b:4096 + 1024 * b].rearrange("p (u s) -> p u s", u=2) for b in range(2)]
        gC = [Y[:, 5120 + 1024 * b:6144 + 1024 * b].rearrange("p (u s) -> p u s", u=2) for b in range(2)]
        wbd = Y[:, 3072:5120].rearrange("p (t r n) -> p t r n", t=8, r=2)
        dtw = Y[:, 2048:2176].rearrange("p (k n) -> p k n", k=KT)
        dtws = Y[:, 2176:2304].bitcast(F16).rearrange("p (h k n) -> p h k n", h=2, k=KT)
        dtri = Y[:, 3072:4096].rearrange("p (j l) -> p j l", j=8)
        est = Y[:, 4096:5120].rearrange("p (j l) -> p j l", j=8)
        xdt, xw, state, yt = (Y[:, 5120 + 512 * i:5632 + 512 * i].rearrange("p (j n) -> p j n", j=8) for i in range(4))
        inter = Y[:, 3072:3584].rearrange("p (j n) -> p j n", j=8)
        gm = Y[:, 7168:7296]
        dtv, dta, cs, ecs, dend, cdec = (Y[:, 7296 + 64 * i:7360 + 64 * i].rearrange("p (c j) -> p c j", c=ST) for i in range(6))
        spw = Y[:, 7680:8400].rearrange("p (i n) -> p i n", n=72)
        ea = Y[:, 8400:8416]
        dE = Y[:, 0:2048].rearrange("p (e t n) -> p e t n", e=2, t=2)
        dA = Y[:, 2048:3072].rearrange("p (e n) -> p e n", e=2)
        dPT = Y[:, 3072:4096].rearrange("p (e n) -> p e n", e=2)
        dO = Y[:, 4096:5120].rearrange("p (n e) -> p n e", n=8)
        dy = Y[:, 5120:6144].rearrange("p (u s) -> p u s", u=2)
        dsq = Y[:, 6144:7168].rearrange("p (n e) -> p n e", n=8)
        pg = Y[:, 0:1024]
        Mseq = M[:, :, :].rearrange("p a b -> p (a b)").rearrange("p (s n) -> p s n", s=ST)
        rowsA, rowsB = X[0:A_N, 0:P], X[0:B_N, P:2 * P]
        ss, rin = small[:, 0:4], small[:, 4:8]
        sm = small[:, 8:16].rearrange("p (e k) -> p e k", e=2)
        sd = small[:, 16:24].rearrange("p (e k) -> p e k", e=2)
        ssum = small[:, 24:32].rearrange("p (e k) -> p e k", e=2)
        srin = small[:, 32:40].rearrange("p (e k) -> p e k", e=2)
        dm = small[:, 40:44].rearrange("p (e t) -> p e t", e=2)
        dsum = small[:, 44:48].rearrange("p (e t) -> p e t", e=2)
        drin = small[:, 48:52].rearrange("p (e t) -> p e t", e=2)
        dss, drs = small[:, 52:60], small[:, 60:68]
        eps = small[:, 68:69]
        nlam, ng2 = small[:, 69:70], small[:, 70:71]
        sp4, nsp4 = small[:, 72:80], small[:, 80:88]
        lsum = small[:, 88:90]
        gss, grin = small[:, 92:96], small[:, 96:100]
        eps2 = small[:, 100:101]

        names = ["consts_in", "x_in", "stored", "cols_in", "rows_in", "wbd_zero", "wbd_in", "dtw_in", "post_in",
                 "load0", "load1", "hi_done", "lo_done", "panel_done", "tile_done", "act_free", "dve_free", "gate_ready",
                 "act_chain", "dve_chain", "pool_chain",
                 "ss_ready", "rin_ready", "xn_ready", "cols_T", "cols_ready", "xn_T", "h_hi", "h_lo",
                 "dtw_hi", "dtw_lo", "dt_raw", "sp_in", "sp_exp", "dta_ready", "cs_done", "cs_ready", "dec_ready", "lru_par",
                 "conv_done", "lru_gates", "lru_a", "lru_v", "lru_w", "lru_a2", "lru_vv", "lru_ww", "lru_beta", "lru_bw",
                 "lru_y", "y_hi", "y_lo", "conv_tanh", "conv_silu", "xt_done", "xt_read",
                 "rope_dma", "rope_sin", "rope_done", "kswap",
                 "ssd_tri", "ssd_x", "ssd_g", "ssd_exp", "ssd_mt", "ssd_y", "ssd_out", "ssd_st", "ssd_ss", "ssd_norm", "ssd_T",
                 "yb_hi", "yb_lo", "sw_s", "sw_m", "sw_e", "sw_n", "sw_T", "sw_Ta", "sw_Tv", "sw_o", "sw_y",
                 "lam_e", "df_s", "df_m", "df_e", "df_a", "df_T", "df_Tr", "df_o", "df_or", "df_ss", "df_sq", "df_n", "df_nT", "df_y",
                 "m_acc", "m_hi", "m_lo", "fin_ss", "fin_sq", "fin_y"]
        s = {n: ctx.enter_context(nc.semaphore(n)) for n in names}
        load = [s["load0"], s["load1"]]

        with nc.Block() as block:
            @block.sync
            def _(sp):
                sp.dma_start(K[:, :], consts).then_inc(s["consts_in"], 16)
                sp.dma_start(xres[:, :, :], x.rearrange("b (s p) n -> p (b s) n", p=P)).then_inc(s["x_in"], 16)
                sp.wait_ge(s["consts_in"], 16)
                sp.wait_ge(s["x_in"], 16)

            @block.vector
            def _(dve):
                dve.memset(eps, EPS)
                dve.memset(eps2, EPS)

        layer_loop = nc.Fori(0, L)
        layer = layer_loop.__enter__()
        block_guard = nc.Block()
        block = block_guard.__enter__()

        @block.sync
        def _(sp):
            def panel_source(p):
                kind, i, which, c0 = PANELS[p]
                if which == "in":
                    src = w_in[bass.ds(layer, 1), :, c0:c0 + PW]
                elif which == "br":
                    src = w_branch[bass.ds(layer * 4 + i // 4, 1), :, c0:c0 + PW]
                else:
                    src = w_out[bass.ds(layer, 1), :, c0:c0 + PW]
                return src.rearrange("a (k p) n -> p (a k) n", p=P)

            def load_panel(p):
                if p >= NS:
                    sp.wait_ge(s["lo_done"], p - NS + 1)
                sp.dma_start(stage[:, p % NS], panel_source(p)).then_inc(load[p % NS], 16)

            sp.dma_start(rowsA, cols_a[bass.ds(layer, 1)].rearrange("a r p -> (a r) p")).then_inc(s["cols_in"], 16)
            sp.dma_start(rowsB, cols_b[bass.ds(layer, 1)].rearrange("a r p -> (a r) p")).then_inc(s["cols_in"], 16)
            load_panel(0)
            sp.dma_start(dtw, w_in[bass.ds(layer, 1), :, C_DT:C_DT + 16]
                         .rearrange("a (k p) n -> p (a k) n", p=P)).then_inc(s["dtw_in"], 16)
            sp.dma_start(rowp[:, :], rows[bass.ds(layer, 1)].rearrange("a b n -> (a b) n").to_broadcast([P, R_N]))\
                .then_inc(s["rows_in"], 16)
            load_panel(1)
            sp.wait_ge(s["wbd_zero"], 1)
            for r, w in enumerate((w_r, w_i)):
                for o in range(2):
                    sp.dma_start(wbd[HD * o:HD * o + HD, :, r, HD * o:HD * o + HD],
                                 w[bass.ds(layer, 1)].rearrange("a (t o) i j -> o i (a t) j", o=2)[o])\
                        .then_inc(s["wbd_in"], 16)
            for p in range(2, NP):
                load_panel(p)
            sp.wait_ge(s["y_lo"], 32)
            sp.dma_start(pg, post_g[bass.ds(layer, 1)].rearrange("a b n -> (a b) n").to_broadcast([P, D]))\
                .then_inc(s["post_in"], 16)

        @block.tensor
        def _(pe):
            def mm(o, a, b, start, stop):
                return pe.matmul(o, a, b, start=start, stop=stop, skip_group_check=True)

            def wait_bank(tile):
                if tile >= 4:
                    if freed_by_vector(tile - 4):
                        pe.wait_ge(s["dve_free"], dve_frees(tile - 4))
                    else:
                        pe.wait_ge(s["act_free"], act_frees(tile - 4))

            def operand(p):
                kind, i, which, _ = PANELS[p]
                if which == "in":
                    if p == 0:
                        pe.wait_ge(s["h_hi"], 8)
                        pe.wait_ge(s["h_lo"], 8)
                    return hT[:, 0], hT[:, 1]
                if which == "br":
                    n = i // 4
                    if n == 1:
                        pe.wait_ge(s["yb_hi"], 8)
                        pe.wait_ge(s["yb_lo"], 8)
                    else:
                        pe.wait_ge(s["y_lo"], {0: 8, 2: 24, 3: 32}[n])
                    return Y_HI[n % 2], Y_LO[n % 2]
                pe.wait_ge(s["m_lo"], 8)
                return Y_HI[0], Y_LO[0]

            def tile_product(p, u):
                b = p % NB
                tile = 2 * p + u
                hi, lo = operand(p)
                if u == 0:
                    pe.wait_ge(s["lo_done"], p + 1)
                    pe.wait_ge(s["hi_done"], p + 1)
                wait_bank(tile)
                bank = PS[:, tile % 4]
                if PANELS[p][0] in ("z", "vc", "vd", "out"):
                    for h in range(2):
                        q = 2 * u + h
                        o = bank[:, PW * h:PW * h + PW]
                        for k in range(KT):
                            a, al = hi[:, k, q * P:q * P + P], lo[:, k, q * P:q * P + P]
                            mm(o, a, wsp[:, b, 0, k, :], k == 0, False)
                            mm(o, a, wsp[:, b, 1, k, :], False, False)
                            last = mm(o, al, wsp[:, b, 0, k, :], False, k == KT - 1)
                else:
                    for k in range(KT):
                        wh, wl = wsp[:, b, 0, k, P * u:P * u + P], wsp[:, b, 1, k, P * u:P * u + P]
                        mm(bank, wh, hi[:, k, :], k == 0, False)
                        mm(bank, wh, lo[:, k, :], False, False)
                        last = mm(bank, wl, hi[:, k, :], False, k == KT - 1)
                last.then_inc(s["tile_done"], 1)

            def before(p):
                if p == 1:
                    pe.wait_ge(s["dta_ready"], 1)
                    d = dta.rearrange("p c j -> p (c j)")
                    mm(PS[:, 5, 0:64], tri, d, True, True)
                    mm(PS[:, 6, 0:64], ones, d, True, True).then_inc(s["cs_done"], 1)
                if p in SSD_SLOT:
                    q = SSD_SLOT.index(p)
                    g, c = divmod(q, 4)
                    if q == 0:
                        pe.wait_ge(s["conv_silu"], 8)
                        pe.wait_ge(s["y_lo"], 8)
                    if q > 0:
                        pe.wait_ge(s["ssd_y"], q)
                        pe.wait_ge(s["ssd_st"], q - (q > 3))
                    if q == 4:
                        pe.wait_ge(s["yb_hi"], 4)
                        pe.wait_ge(s["yb_lo"], 4)
                    pe.wait_ge(s["xt_read"], min(10, 2 + conv_tiles(p) - 12 - 2 * (PANELS[p - 1][0] == "conv")))
                    mm(PS[:, 4, 0:P], BT[:, g, c * P:c * P + P], CT[:, g, c * P:c * P + P], True, True)
                    pe.wait_ge(s["ssd_tri"], q + 1)
                    for h in range(2):
                        last = mm(PS[:, 5 + h, :], strict, dtri[:, 4 * h:4 * h + 4, :].rearrange("p j l -> p (j l)"), True, True)
                    last.then_inc(s["ssd_g"], 1)
                if SWA0 <= p < SWA0 + 8:
                    for e in range(2):
                        n = 2 * (p - SWA0) + e
                        j, i = divmod(n, 4)
                        if n == 0:
                            pe.wait_ge(s["kswap"], 32)
                            pe.wait_ge(s["yb_hi"], 8)
                            pe.wait_ge(s["yb_lo"], 8)
                        if i == 0:
                            pe.wait_ge(s["rope_done"], 2 + j)
                        if n >= 2:
                            pe.wait_ge(s["sw_y"], n - 1)
                        k0 = 0 if i else P
                        for r in range(4):
                            at = HD * (r % 2)
                            keys = (kC if j % 2 == r % 2 else kCs)[at:at + HD, j // 2, (i - 1) * P + k0:(i + 1) * P]
                            o = PS[:, 4 + 2 * e + r % 2, PW * (r // 2) + k0:PW * (r // 2) + PW]
                            mm(o, qC[j % 2][at:at + HD, r // 2, i * P:i * P + P], keys, True, False)
                            last = mm(o, K[at:at + HD, K_ML:K_ML + P], K[at:at + HD, K_MR + k0:K_MR + PW], False, True)
                        last.then_inc(s["sw_s"], 1)
                if DIFF0 <= p < DIFF0 + 16:
                    for e in range(2):
                        n = 2 * (p - DIFF0) + e
                        h2, u, i = n // 8, (n // 4) % 2, n % 4
                        if n % 8 == 0:
                            pe.wait_ge(s["rope_done"], 7 + 2 * h2)
                        if n == 0:
                            pe.wait_ge(s["sw_y"], 16)
                        if n >= 2:
                            pe.wait_ge(s["df_or"], n - 1)
                        if n % 8 < 2 and h2 > 1:
                            pe.wait_ge(s["df_y"], 2 * h2 - 2)
                        if n % 8 in (2, 3) and h2 > 0:
                            pe.wait_ge(s["df_y"], 2 * h2)
                        for t in range(2):
                            at = HD * t
                            o = PS[:, 4 + 2 * e + t, 0:(i + 1) * P]
                            mm(o, qD[h2 % 2][at:at + HD, u, i * P:i * P + P], kD[h2 % 2][at:at + HD, u, 0:(i + 1) * P], True, False)
                            last = mm(o[:, i * P:i * P + P], K[at:at + HD, K_ML:K_ML + P],
                                      K[at:at + HD, K_MR + P:K_MR + PW], False, True)
                        last.then_inc(s["df_s"], 1)

            def between(p):
                if p > 0 and PANELS[p - 1][0] == "conv" and PANELS[p - 1][1] != 10:
                    i = PANELS[p - 1][1]
                    for u in range(2):
                        n = [8, 0, 2, 4, 6].index(i) * 2 + u
                        pe.wait_ge(s["conv_silu"], conv_tiles(p) - 8 - 1 + u)
                        if n == 0:
                            pe.wait_ge(s["y_lo"], 8)
                        if n >= 2:
                            pe.wait_ge(s["xt_read"], n - 1)
                        if p in SSD_SLOT:
                            pe.wait_ge(s["ssd_exp"], SSD_SLOT.index(p) + 1)
                        src = BT[:, u, :] if i == 8 else wbuf[:, u, :]
                        for q in range(ST):
                            last = pe.transpose(PS[:, 6 + u, q * P:q * P + P], src[:, q * P:q * P + P], ident)
                        last.then_inc(s["xt_done"], 1)
                if p in SSD_SLOT:
                    q = SSD_SLOT.index(p)
                    g, c = divmod(q, 4)
                    pe.wait_ge(s["ssd_mt"], q + 1)
                    pe.wait_ge(s["ssd_x"], q + 1)
                    if PANELS[p - 1][0] == "conv":
                        pe.wait_ge(s["xt_read"], conv_tiles(p) - 8 - 2)
                    for j in range(8):
                        mm(PS[:, 4, HD * j:HD * j + HD], est[:, j, :], xdt[:, j, :], True, True)
                    if c > 0:
                        pe.wait_ge(s["ssd_st"], 3 * g + c)
                        last = mm(PS[:, 7, :], CT[:, g, c * P:c * P + P], state.rearrange("p j n -> p (j n)"), True, True)
                    if c < 3:
                        last = mm(PS[:, 5, :], Bseq[:, c, g * P:g * P + P], xw.rearrange("p j n -> p (j n)"), True, True)
                    last.then_inc(s["ssd_out"], 1)
                if p in SSD_END:
                    g = SSD_END[p]
                    pe.wait_ge(s["ssd_norm"], g + 1)
                    pe.wait_ge(s["ssd_y"], 4 * g + 4)
                    for t in range(4):
                        for c in range(ST):
                            last = pe.transpose(PS[:, 4 + t, c * P:c * P + P], z[g][:, c, t * P:t * P + P], ident)
                        last.then_inc(s["ssd_T"], 1)
                if SWA0 <= p < SWA0 + 8:
                    for e in range(2):
                        n = 2 * (p - SWA0) + e
                        pe.wait_ge(s["sw_n"], n + 1)
                        for k in range(4):
                            for b in range(0 if n % 4 else 1, 2):
                                last = pe.transpose(PS[:, 4 + 2 * e + k // 2, PW * (k % 2) + P * b:PW * (k % 2) + P * b + P],
                                                    sE[:, e, k, P * b:P * b + P], ident)
                        last.then_inc(s["sw_T"], 1)
                if DIFF0 <= p < DIFF0 + 16:
                    for e in range(2):
                        n = 2 * (p - DIFF0) + e
                        pe.wait_ge(s["df_a"], n + 1)
                        for b in range(n % 4 + 1):
                            last = pe.transpose(PS[:, 4 + 2 * e, P * b:P * b + P], dA[:, e, P * b:P * b + P], ident)
                        last.then_inc(s["df_T"], 1)

            def after(p):
                if PANELS[p][0] == "ga":
                    for u in range(2):
                        t = 2 * PANELS[p][1] + u
                        if t == 0:
                            pe.wait_ge(s["wbd_in"], 64)
                            pe.wait_ge(s["dec_ready"], 1)
                        if t >= 2:
                            pe.wait_ge(s["lru_w"], t - 1)
                            pe.wait_ge(s["lru_v"], t - 1)
                        pe.wait_ge(s["conv_done"], t + 1)
                        mm(PS[:, 4 + 2 * u, :], wbd[:, t, 0, :], cbuf[:, u, :], True, True)
                        mm(PS[:, 5 + 2 * u, :], wbd[:, t, 1, :], cbuf[:, u, :], True, True).then_inc(s["lru_gates"], 1)
                if SWA0 <= p < SWA0 + 8:
                    for e in range(2):
                        n = 2 * (p - SWA0) + e
                        j, i = divmod(n, 4)
                        pe.wait_ge(s["sw_Ta"], n + 1)
                        pe.wait_ge(s["sw_Tv"], n + 1)
                        for k in range(4):
                            r = 2 * (k % 2) + k // 2
                            o = PS[HD * (r % 2):HD * (r % 2) + HD, 4 + 2 * e, P * (r // 2):P * (r // 2) + P]
                            if i:
                                mm(o, vC[:, i - 1, HD * j:HD * j + HD], sPT[:, e, k, 0:P], True, False)
                            last = mm(o, vC[:, i, HD * j:HD * j + HD], sPT[:, e, k, P:PW], i == 0, True)
                        last.then_inc(s["sw_o"], 1)
                if p in DIFF_END:
                    h2 = DIFF_END[p]
                    pe.wait_ge(s["df_n"], h2 + 1)
                    for u in range(2):
                        if p < DIFF0 + 16:
                            pe.wait_ge(s["df_Tr"], 2 * (p - DIFF0) + 1 + u)
                        for i in range(4):
                            last = pe.transpose(PS[:, 4 + 2 * u, P * i:P * i + P], dO[:, 4 * u + i, :], ident)
                        last.then_inc(s["df_nT"], 1)
                if DIFF0 <= p < DIFF0 + 16:
                    for e in range(2):
                        n = 2 * (p - DIFF0) + e
                        h2, u, i = n // 8, (n // 4) % 2, n % 4
                        pe.wait_ge(s["df_Tr"], n + 1)
                        for b in range(i + 1):
                            last = mm(PS[:, 5 + 2 * e, 0:P], dPT[:, e, P * b:P * b + P], vD[h2 % 2][:, b, P * u:P * u + P],
                                      b == 0, b == i)
                        last.then_inc(s["df_o"], 1)

            pe.wait_ge(s["cols_in"], 32)
            pe.transpose(PS[:, 0, 0:A_N], rowsA, ident[0:A_N, 0:A_N])
            pe.transpose(PS[:, 1, 0:B_N], rowsB, ident[0:B_N, 0:B_N]).then_inc(s["cols_T"], 1)
            pe.wait_ge(s["cols_ready"], 2)
            for k in range(KT):
                for q in range(ST):
                    if k == 0:
                        pe.wait_ge(s["xn_ready"], q + 1)
                    last = pe.transpose(PS[:, k, q * P:q * P + P], Mseq[:, q, k * P:k * P + P], ident)
                last.then_inc(s["xn_T"], 1)
            pe.wait_ge(s["h_hi"], 8)
            pe.wait_ge(s["h_lo"], 8)
            pe.wait_ge(s["dtw_hi"], 1)
            pe.wait_ge(s["dtw_lo"], 1)
            for q in range(ST):
                for k in range(KT):
                    o = PS[:, 4, 16 * q:16 * q + 16]
                    mm(o, hT[:, 0, k, q * P:q * P + P], dtws[:, 0, k, :], k == 0, False)
                    mm(o, hT[:, 0, k, q * P:q * P + P], dtws[:, 1, k, :], False, False)
                    last = mm(o, hT[:, 1, k, q * P:q * P + P], dtws[:, 0, k, :], False, k == KT - 1)
            last.then_inc(s["dt_raw"], 1)
            for p in range(NP):
                before(p)
                tile_product(p, 0)
                between(p)
                tile_product(p, 1)
                after(p)

        @block.scalar
        def _(act):
            chain = [0]

            def link(ins):
                chain[0] += 1
                ins.then_inc(s["act_chain"], 1)
                act.wait_ge(s["act_chain"], chain[0])

            def split_hi(p):
                act.wait_ge(load[p % NS], 16 * (p // NS + 1))
                if p >= NB:
                    act.wait_ge(s["tile_done"], 2 * (p - NB + 1))
                act.activation(wsp[:, p % NB, 0], stage[:, p % NS], ACT.Copy, scale=WS).then_inc(s["hi_done"], 1)

            def copy(o, i, scale=1.0):
                return act.activation(o, i, ACT.Copy, scale=scale)

            def evacuate(p):
                kind, i, _, _ = PANELS[p]
                for u in range(2):
                    tile = 2 * p + u
                    bank = PS[:, tile % 4]
                    act.wait_ge(s["tile_done"], tile + 1)
                    if kind in ("ga", "z", "gc", "gd", "mg"):
                        n = gate_writes(tile)
                        if n >= 2:
                            act.wait_ge(s["dve_free"], n - 1)
                        if kind == "mg":
                            bm = halfA[:, A_BM + 2 * i + u:A_BM + 2 * i + u + 1]
                            act.activation(G[:, u], bank, ACT.Tanh, scale=0.5 * IWS, bias=bm).then_inc(s["act_free"], 1)
                        else:
                            act.activation(G[:, u], bank, ACT.Tanh, scale=0.5 * IWS).then_inc(s["gate_ready"], 1)
                    elif kind in ("xa", "conv"):
                        n = conv_tiles(p) + u
                        if n >= 2:
                            act.wait_ge(s["conv_done"], n - 1)
                        copy(xpad[:, u, 3:3 + S], bank, IWS).then_inc(s["act_free"], 1)
                    elif kind in ("kc", "qc", "qd", "kd"):
                        n = rope_index(p)
                        if n >= 1:
                            act.wait_ge(s["rope_done"], n)
                        if kind == "qd" and i == 0:
                            act.wait_ge(s["y_lo"], 24)
                        copy(rraw[:, u, :], bank, IWS if kind in ("kc", "kd") else IWS / 8).then_inc(s["act_free"], 1)
                    elif kind in ("vc", "vd"):
                        if kind == "vd" and i >= 2:
                            act.wait_ge(s["df_o"], 8 * (i - 1))
                        dst = vC if kind == "vc" else vD[i % 2]
                        copy(dst[:, 2 * u:2 * u + 2, :].rearrange("p c n -> p (c n)"), bank, IWS).then_inc(s["act_free"], 1)
                    elif kind == "out":
                        copy(Mseq[:, 2 * u:2 * u + 2, PW * i:PW * i + PW], bank.rearrange("p (h n) -> p h n", h=2), IWS)\
                            .then_inc(s["act_free"], 1)

                if kind in ("kc", "qc", "qd", "kd"):
                    act.wait_ge(s["act_free"], act_frees(2 * p + 1))
                    for a, b in ((0, 32), (32, 0), (64, 96), (96, 64)):
                        act.dma_start(rswap[a:a + 32], rraw[b:b + 32]).then_inc(s["rope_dma"], 16)

            def before(p):
                if p > 0 and PANELS[p - 1][0] == "vc":
                    act.wait_ge(s["rope_done"], 1)
                    for a, b in ((0, HD), (HD, 0)):
                        act.dma_start(kCs[a:a + HD], kC[b:b + HD]).then_inc(s["kswap"], 16)
                if p == 0:
                    act.wait_ge(s["sp_in"], 1)
                    link(act.activation(ea, rowp[:, R_AL:R_AL + 16], ACT.Exp))
                    act.activation(spw[:, 2, :], spw[:, 1, :], ACT.Exp).then_inc(s["sp_exp"], 1)
                    act.wait_ge(s["lam_e"], 1)
                    act.activation(lsum, lsum, ACT.Exp).then_inc(s["lam_e"], 1)
                if p == 1:
                    act.wait_ge(s["cs_done"], 1)
                    act.wait_ge(s["cs_ready"], 1)
                    act.activation(ecs.rearrange("p c j -> p (c j)"), PS[:, 5, 0:64], ACT.Exp)
                    link(act.activation(cdec.rearrange("p c j -> p (c j)"), PS[:, 6, 0:64], ACT.Exp))
                    act.activation(dend.rearrange("p c j -> p (c j)"), dend.rearrange("p c j -> p (c j)"), ACT.Exp)\
                        .then_inc(s["dec_ready"], 1)
                if p > 0 and PANELS[p - 1][0] == "ga":
                    j = PANELS[p - 1][1]
                    act.wait_ge(s["lru_par"], 1)
                    for u in range(2):
                        t = 2 * j + u
                        act.wait_ge(s["lru_gates"], t + 1)
                        link(act.activation(rbuf[:, u, :], PS[:, 4 + 2 * u], ACT.Tanh, scale=0.5, bias=halfA[:, A_BR + t:A_BR + t + 1]))
                        act.activation(abuf[:, u, :], rbuf[:, u, :], ACT.Exp, scale=nsp4[:, t:t + 1], bias=nsp4[:, t:t + 1])\
                            .then_inc(s["lru_a"], 1)
                        act.activation(vbuf[:, u, :], rbuf[:, u, :], ACT.Tanh, scale=sp4[:, t:t + 1], bias=sp4[:, t:t + 1])\
                            .then_inc(s["lru_v"], 1)
                        act.activation(wbuf[:, u, :], PS[:, 5 + 2 * u], ACT.Tanh, scale=0.5, bias=halfA[:, A_BI + t:A_BI + t + 1])\
                            .then_inc(s["lru_w"], 1)
                    act.wait_ge(s["lru_vv"], 2 * j + 2)
                    act.activation(vbuf, vbuf, ACT.Sqrt).then_inc(s["lru_beta"], 1)
                    for u in range(2):
                        t = 2 * j + u
                        act.wait_ge(s["lru_y"], t + 1)
                        copy(Y_HI[0][:, t, :], hbuf[:, u, :]).then_inc(s["y_hi"], 1)
                if p > 0 and PANELS[p - 1][0] == "conv":
                    for u in range(2):
                        n = conv_tiles(p - 1) + u
                        act.wait_ge(s["conv_done"], n + 1)
                        if n - 8 >= 2:
                            act.wait_ge(s["conv_silu"], n - 8 - 1)
                        act.activation(rbuf[:, u, :], cbuf[:, u, :], ACT.Tanh, scale=0.5).then_inc(s["conv_tanh"], 1)
                if p in SSD_SLOT:
                    q = SSD_SLOT.index(p)
                    act.wait_ge(s["ssd_g"], q + 1)
                    if q > 0:
                        act.wait_ge(s["ssd_out"], q)
                    act.activation(est.rearrange("p j l -> p (j l)"), PS[:, 5:7, :].rearrange("p b n -> p (b n)"), ACT.Exp)\
                        .then_inc(s["ssd_exp"], 1)
                if p in SSD_END:
                    g = SSD_END[p]
                    act.wait_ge(s["ssd_y"], 4 * g + 4)
                    for c in range(ST):
                        link(act.activation(est.rearrange("p j l -> p (j l)")[:, 0:S], z[g][:, c, :], ACT.Square,
                                            accum_out=gss[:, c:c + 1]))
                    act.activation(gss, gss, ACT.Sqrt, scale=1.0 / (512 * P * P), bias=eps).then_inc(s["ssd_ss"], 1)
                if SWA0 <= p < SWA0 + 8:
                    for e in range(2):
                        n = 2 * (p - SWA0) + e
                        k0 = 0 if n % 4 else P
                        act.wait_ge(s["sw_m"], n + 1)
                        if n >= 2:
                            act.wait_ge(s["sw_T"], n - 1)
                        for k in range(4):
                            act.activation(sE[:, e, k, k0:PW], PS[:, 4 + 2 * e + k // 2, PW * (k % 2) + k0:PW * (k % 2) + PW],
                                           ACT.Exp, bias=sm[:, e, k:k + 1], accum_out=ssum[:, e, k:k + 1])
                        act.activation(sd[:, e], sd[:, e], ACT.Exp).then_inc(s["sw_e"], 1)
                if DIFF0 <= p < DIFF0 + 16:
                    for e in range(2):
                        n = 2 * (p - DIFF0) + e
                        nk = (n % 4 + 1) * P
                        act.wait_ge(s["df_m"], n + 1)
                        act.activation(dE[:, e, 0, 0:nk], PS[:, 4 + 2 * e, 0:nk], ACT.Exp, bias=dm[:, e, 0:1], accum_out=dsum[:, e, 0:1])
                        link(act.activation(dE[:, e, 1, 0:nk], PS[:, 5 + 2 * e, 0:nk], ACT.Exp, bias=dm[:, e, 1:2],
                                            accum_out=dsum[:, e, 1:2]))
                        act.activation(dsum[:, e], dsum[:, e], ACT.Copy).then_inc(s["df_e"], 1)
                if p in DIFF_END:
                    act.wait_ge(s["df_ss"], DIFF_END[p] + 1)
                    act.activation(dss, dss, ACT.Sqrt, scale=1.0 / P, bias=eps).then_inc(s["df_sq"], 1)

            def between(p):
                if p > 0 and PANELS[p - 1][0] == "conv" and PANELS[p - 1][1] != 10:
                    i = PANELS[p - 1][1]
                    for u in range(2):
                        n = [8, 0, 2, 4, 6].index(i) * 2 + u
                        act.wait_ge(s["xt_done"], n + 1)
                        src = PS[:, 6 + u, :].rearrange("p (c n) -> p c n", c=ST)
                        if i == 8:
                            copy(Bseq[:, :, P * u:P * u + P], src).then_inc(s["xt_read"], 1)
                        else:
                            t = (i + u) % 4
                            copy(xs[i // 4][:, :, P * t:P * t + P], src, 0.5).then_inc(s["xt_read"], 1)
                if p in SSD_END:
                    g = SSD_END[p]
                    for t in range(4):
                        f = 4 * g + t
                        act.wait_ge(s["ssd_T"], f + 1)
                        copy(Y_HI[1][:, f, :], PS[:, 4 + t, :], colB[:, B_NG + f:B_NG + f + 1]).then_inc(s["yb_hi"], 1)
                if SWA0 <= p < SWA0 + 8:
                    for e in range(2):
                        n = 2 * (p - SWA0) + e
                        k0 = 0 if n % 4 else P
                        act.wait_ge(s["sw_T"], n + 1)
                        if n >= 2:
                            act.wait_ge(s["sw_o"], n - 1)
                        copy(sPT[:, e, 2:4, k0:PW], PS[:, 5 + 2 * e, :].rearrange("p (k n) -> p k n", k=2)[:, :, k0:PW])\
                            .then_inc(s["sw_Ta"], 1)
                if DIFF0 <= p < DIFF0 + 16:
                    for e in range(2):
                        n = 2 * (p - DIFF0) + e
                        nk = (n % 4 + 1) * P
                        act.wait_ge(s["df_T"], n + 1)
                        if n >= 2:
                            act.wait_ge(s["df_o"], n - 1)
                        copy(dPT[:, e, 0:nk], PS[:, 4 + 2 * e, 0:nk]).then_inc(s["df_Tr"], 1)

            def after(p):
                if SWA0 <= p < SWA0 + 8:
                    for e in range(2):
                        n = 2 * (p - SWA0) + e
                        j, i = divmod(n, 4)
                        act.wait_ge(s["sw_y"], n + 1)
                        if n == 0:
                            act.wait_ge(s["tile_done"], 2 * (SLOT[("br", 3)] + 1))
                        copy(Y_HI[0][:, 2 * j:2 * j + 2, i * P:i * P + P], sy[:, e]).then_inc(s["y_hi"], 1)
                if p in DIFF_END:
                    h2 = DIFF_END[p]
                    act.wait_ge(s["df_nT"], 2 * h2 + 2)
                if DIFF0 <= p < DIFF0 + 16:
                    for e in range(2):
                        n = 2 * (p - DIFF0) + e
                        act.wait_ge(s["df_o"], n + 1)
                        copy(dO[:, n % 8, :], PS[:, 5 + 2 * e, 0:P]).then_inc(s["df_or"], 1)
                if p in DIFF_END:
                    h2 = DIFF_END[p]
                    for u in range(2):
                        act.wait_ge(s["df_y"], 2 * h2 + u + 1)
                        if h2 == 0 and u == 0:
                            act.wait_ge(s["tile_done"], 2 * (SLOT[("br", 7)] + 1))
                        copy(Y_HI[1][:, 2 * h2 + u, :], dy[:, u, :]).then_inc(s["y_hi"], 1)
                if PANELS[p][0] == "br" and PANELS[p][1] >= 12:
                    i = PANELS[p][1] - 12
                    for u in range(2):
                        act.wait_ge(s["m_acc"], 16 + 2 * i + u + 1)
                        if i == 0 and u == 0:
                            act.wait_ge(s["tile_done"], 2 * (SLOT[("br", 11)] + 1))
                        copy(Y_HI[0][:, 2 * i + u, :], M[:, 2 * i + u, :], 1.0 / P).then_inc(s["m_hi"], 1)

            def root_of_squares(o, rows_of, scratch, finished):
                for q in range(ST):
                    link(act.activation(scratch, rows_of(q), ACT.Square, accum_out=o[:, q:q + 1]))
                act.activation(o, o, ACT.Sqrt, scale=1.0 / D, bias=eps).then_inc(finished, 1)

            junk = Y[:, 0:1024]
            root_of_squares(ss, lambda q: xres[:, q, :], junk, s["ss_ready"])
            act.wait_ge(s["cols_T"], 1)
            copy(colA[:, :], PS[:, 0, 0:A_N]).then_inc(s["cols_ready"], 1)
            copy(colB[:, :], PS[:, 1, 0:B_N]).then_inc(s["cols_ready"], 1)
            act.wait_ge(s["cols_ready"], 2)
            for k in range(KT):
                act.wait_ge(s["xn_T"], k + 1)
                copy(hT[:, 0, k, :], PS[:, k, :], colA[:, A_G + k:A_G + k + 1]).then_inc(s["h_hi"], 1)
            act.wait_ge(s["dtw_in"], 16)
            copy(dtws[:, 0], dtw, WS).then_inc(s["dtw_hi"], 1)
            split_hi(0)
            for p in range(NP):
                if p + 1 < NP:
                    split_hi(p + 1)
                before(p)
                between(p)
                evacuate(p)
                after(p)
            act.wait_ge(s["act_free"], act_frees(2 * NP - 1))
            root_of_squares(ss, lambda q: Mseq[:, q, :], Y[:, 1024:2048], s["fin_ss"])

        @block.vector
        def _(dve):
            chain = [0]

            def link(ins):
                chain[0] += 1
                ins.then_inc(s["dve_chain"], 1)
                dve.wait_ge(s["dve_chain"], chain[0])

            def stt(o, a, c, b, op0, op1):
                return dve.scalar_tensor_tensor(out=o, in0=a, scalar=c, in1=b, op0=op0, op1=op1)

            def tt(o, a, b, op):
                return dve.tensor_tensor(o, a, b, op)

            def split_lo(p):
                dve.wait_ge(s["hi_done"], p + 1)
                stt(wsp[:, p % NB, 1].rearrange("p k n -> p (k n)"), stage[:, p % NS].rearrange("p k n -> p (k n)"), WS,
                    wsp[:, p % NB, 0].rearrange("p k n -> p (k n)"), ALU.mult, ALU.subtract).then_inc(s["lo_done"], 1)

            def convolve(u, weights, col, step, bias):
                w = [weights[:, col + step * k:col + step * k + 1] for k in range(4)]
                link(dve.tensor_scalar(cbuf[:, u, :], xpad[:, u, 3:3 + S], w[3], bias, ALU.mult, ALU.add))
                for k in (2, 1):
                    link(stt(cbuf[:, u, :], xpad[:, u, k:k + S], w[k], cbuf[:, u, :], ALU.mult, ALU.add))
                stt(cbuf[:, u, :], xpad[:, u, 0:S], w[0], cbuf[:, u, :], ALU.mult, ALU.add).then_inc(s["conv_done"], 1)
                dve.wait_ge(s["conv_done"], conv_count[0] + 1)
                conv_count[0] += 1

            conv_count = [0]

            def evacuate(p):
                kind, i, _, _ = PANELS[p]
                for u in range(2):
                    tile = 2 * p + u
                    bank = PS[:, tile % 4]
                    if kind in ("ga", "z", "gc", "gd"):
                        dve.wait_ge(s["gate_ready"], gate_uses(tile))
                        if kind == "ga":
                            dst, g, b = gbuf[:, u, :], G[:, u], bank
                        elif kind == "z":
                            dst = z[i // 2][:, 2 * u:2 * u + 2, PW * (i % 2):PW * (i % 2) + PW]
                            g, b = G[:, u].rearrange("p (c n) -> p c n", c=2), bank.rearrange("p (c n) -> p c n", c=2)
                        else:
                            dst, g, b = (gC if kind == "gc" else gD)[i % 2][:, u, :], G[:, u], bank
                        stt(dst, g, 1.0, b, ALU.add, ALU.mult).then_inc(s["dve_free"], 1)
                    elif kind in ("xa", "conv"):
                        dve.wait_ge(s["act_free"], act_frees(tile))
                        if kind == "xa":
                            t = 2 * i + u
                            convolve(u, colA, A_CW + t, 8, colA[:, A_CB + t:A_CB + t + 1])
                        else:
                            t = i + u
                            convolve(u, colB, B_CW + t, 12, colB[:, B_CB + t:B_CB + t + 1])
                    elif kind == "br":
                        dve.wait_ge(s["act_free"], act_frees(tile - 2))
                        dve.wait_ge(s["tile_done"], tile + 1)
                        if i < 4:
                            dst = M[:, 2 * i + u, :]
                        else:
                            n = 2 * (i - 4) + u
                            if n >= 2:
                                dve.wait_ge(s["m_acc"], n - 1)
                            dst = T[:, S * u:S * u + S]
                        stt(dst, G[:, u], 1.0, bank, ALU.add, ALU.mult).then_inc(s["dve_free"], 1)
                if kind in ("kc", "qc", "qd", "kd"):
                    dve.wait_ge(s["act_free"], act_frees(2 * p + 1))
                    link(tt(rcos, rraw, cosT.unsqueeze(1).to_broadcast([P, 2, S]), ALU.mult))

            def softplus():
                v, na, e, r, u, q, t, rl, sp_ = (spw[:, i, :] for i in range(9))
                link(dve.tensor_scalar(na, v, -1.0, None, ALU.mult))
                link(tt(na, na, v, ALU.min))
                dve.tensor_scalar(rl, v, 0.0, None, ALU.max).then_inc(s["sp_in"], 1)
                dve.wait_ge(s["sp_in"], 1)
                dve.wait_ge(s["sp_exp"], 1)
                link(dve.tensor_scalar(r, e, 2.0, None, ALU.add))
                link(dve.reciprocal(r, r))
                link(tt(u, e, r, ALU.mult))
                link(tt(q, u, u, ALU.mult))
                link(dve.tensor_scalar(t, q, 1.0 / 13, None, ALU.mult))
                for k in (11, 9, 7, 5, 3):
                    link(stt(t, t, 1.0 / k, q, ALU.add, ALU.mult))
                link(stt(t, t, 1.0, u, ALU.add, ALU.mult))
                link(stt(sp_, t, 2.0, rl, ALU.mult, ALU.add))
                return sp_

            def ssd_triangle(q):
                g, c = divmod(q, 4)
                if q > 0:
                    dve.wait_ge(s["ssd_g"], q)
                if q == 0:
                    dve.wait_ge(s["lru_gates"], 8)
                tt(dtri, tri.unsqueeze(1).to_broadcast([P, 8, P]),
                   dta[:, c, 8 * g:8 * g + 8].unsqueeze(2).to_broadcast([P, 8, P]), ALU.mult).then_inc(s["ssd_tri"], 1)

            def before(p):
                if p == 0:
                    dve.wait_ge(s["dt_raw"], 1)
                    dve.wait_ge(s["rows_in"], 16)
                    bias = rowp[:, R_DTB:R_DTB + 16].unsqueeze(1).to_broadcast([P, ST, 16])
                    link(stt(spw[:, 0, 0:64].rearrange("p (c j) -> p c j", c=ST), PS[:, 4, 0:64].rearrange("p (c j) -> p c j", c=ST),
                             IWS, bias, ALU.mult, ALU.add))
                    link(dve.tensor_scalar(spw[:, 0, 64:72], colA[:, A_LAM:A_LAM + 8], -1.0, None, ALU.mult))
                    sp_ = softplus()
                    link(dve.tensor_copy(dtv.rearrange("p c j -> p (c j)"), sp_[:, 0:64]))
                    stt(dta, dtv, -1.0, ea.unsqueeze(1).to_broadcast([P, ST, 16]), ALU.mult, ALU.mult).then_inc(s["dta_ready"], 1)
                    link(dve.tensor_scalar(sp4, sp_[:, 64:72], 4.0, None, ALU.mult))
                    dve.tensor_scalar(nsp4, sp_[:, 64:72], -4.0, None, ALU.mult).then_inc(s["lru_par"], 1)
                    prod = spw[:, 8:10, :].rearrange("p i n -> p (i n)")[:, 0:128].rearrange("p (i n) -> p i n", i=2)
                    lq = rowp[:, R_LQ:R_LQ + 256].rearrange("p (i t n) -> p i t n", i=2, t=2)
                    dve.wait_ge(s["dta_ready"], 1)
                    dve.wait_ge(s["lru_par"], 1)
                    link(tt(prod, lq[:, :, 0, :], lq[:, :, 1, :], ALU.mult))
                    dve.tensor_reduce(lsum, prod, AX, ALU.add).then_inc(s["lam_e"], 1)
                    dve.wait_ge(s["lam_e"], 2)
                    link(tt(nlam, lsum[:, 1:2], lsum[:, 0:1], ALU.subtract))
                    link(tt(nlam, nlam, rowp[:, R_LI:R_LI + 1], ALU.subtract))
                    link(stt(ng2, colB[:, B_DG:B_DG + 1], 1.0 / P, rowp[:, R_LI + 1:R_LI + 2], ALU.mult, ALU.mult))
                    link(dve.memset(xpad[:, :, 0:3], 0.0))
                if p == 1:
                    dve.wait_ge(s["cs_done"], 1)
                    link(dve.tensor_copy(cs.rearrange("p c j -> p (c j)"), PS[:, 5, 0:64]))
                    tt(dend.rearrange("p c j -> p (c j)"), PS[:, 6, 0:64], cs.rearrange("p c j -> p (c j)"), ALU.subtract)\
                        .then_inc(s["cs_ready"], 1)
                if p > 0 and PANELS[p - 1][0] == "ga":
                    j = PANELS[p - 1][1]
                    for u in range(2):
                        t = 2 * j + u
                        dve.wait_ge(s["lru_a2"], t + 1)
                        stt(vbuf[:, u, :], rbuf[:, u, :], 1.0, vbuf[:, u, :], ALU.add, ALU.mult).then_inc(s["lru_vv"], 1)
                        dve.wait_ge(s["lru_w"], t + 1)
                        stt(wbuf[:, u, :], wbuf[:, u, :], 1.0, cbuf[:, u, :], ALU.add, ALU.mult).then_inc(s["lru_ww"], 1)
                    for u in range(2):
                        t = 2 * j + u
                        dve.wait_ge(s["lru_bw"], t + 1)
                        if t >= 2:
                            dve.wait_ge(s["y_lo"], t - 1)
                        link(dve.tensor_tensor_scan(hbuf[:, u, :], abuf[:, u, :], wbuf[:, u, :], 0.0, ALU.mult, ALU.add))
                        stt(hbuf[:, u, :], hbuf[:, u, :], 1.0 / 256, gbuf[:, u, :], ALU.mult, ALU.mult).then_inc(s["lru_y"], 1)
                if p > 0 and PANELS[p - 1][0] == "conv":
                    i = PANELS[p - 1][1]
                    for u in range(2):
                        n = conv_tiles(p - 1) + u - 8
                        dve.wait_ge(s["conv_tanh"], n + 1)
                        if i >= 8:
                            dst = (BT if i == 8 else CT)[:, u, :]
                            link(stt(dst, rbuf[:, u, :], 1.0, cbuf[:, u, :], ALU.add, ALU.mult))
                            dve.tensor_scalar(dst, dst, 0.5, None, ALU.mult).then_inc(s["conv_silu"], 1)
                        else:
                            if n >= 6:
                                dve.wait_ge(s["xt_done"], n - 3)
                            stt(wbuf[:, u, :], rbuf[:, u, :], 1.0, cbuf[:, u, :], ALU.add, ALU.mult).then_inc(s["conv_silu"], 1)
                if p > 0 and PANELS[p - 1][0] in ("kc", "qc", "qd", "kd"):
                    kind, i = PANELS[p - 1][0:2]
                    n = rope_index(p - 1)
                    dst = {"kc": kC, "qc": qC[i % 2], "qd": qD[i % 2], "kd": kD[i % 2]}[kind]
                    if kind == "qc" and i >= 2:
                        dve.wait_ge(s["sw_s"], 4 * (i - 1))
                    if kind in ("qd", "kd") and i >= 2:
                        dve.wait_ge(s["df_s"], 8 * (i - 1))
                    if kind == "qc" and i == 0:
                        dve.wait_ge(s["ssd_out"], 8)
                    dve.wait_ge(s["rope_sin"], n + 1)
                    tt(dst, rcos, rswap, ALU.add).then_inc(s["rope_done"], 1)
                if p in SSD_SLOT:
                    q = SSD_SLOT.index(p)
                    dve.wait_ge(s["ssd_g"], q + 1)
                    link(tt(gm, PS[:, 4, 0:P], tri, ALU.mult))
                    dve.wait_ge(s["ssd_exp"], q + 1)
                    tt(est, est, gm.unsqueeze(1).to_broadcast([P, 8, P]), ALU.mult).then_inc(s["ssd_mt"], 1)
                if p in SSD_END:
                    g = SSD_END[p]
                    dve.wait_ge(s["ssd_ss"], g + 1)
                    link(dve.reciprocal(grin, gss))
                    link(dve.tensor_scalar(grin, grin, 1.0 / P, None, ALU.mult))
                    tt(z[g], z[g], grin.unsqueeze(2).to_broadcast([P, ST, S]), ALU.mult).then_inc(s["ssd_norm"], 1)
                if p in DIFF_END:
                    h2 = DIFF_END[p]
                    dve.wait_ge(s["df_or"], 8 * h2 + 8)
                    link(tt(dsq, dO, dO, ALU.mult))
                    dve.tensor_reduce(dss, dsq, AX, ALU.add).then_inc(s["df_ss"], 1)
                if SWA0 <= p < SWA0 + 8:
                    for e in range(2):
                        n = 2 * (p - SWA0) + e
                        j = n // 4
                        k0 = 0 if n % 4 else P
                        sink = rowp[:, R_SINK + 4 * j:R_SINK + 4 * j + 4].rearrange("p (s b) -> p b s", b=2)
                        m, d = (v[:, e].rearrange("p (b s) -> p b s", b=2) for v in (sm, sd))
                        dve.wait_ge(s["sw_s"], n + 1)
                        scores = PS[:, 4 + 2 * e:6 + 2 * e, :].rearrange("p b (s n) -> p b s n", s=2)[:, :, :, k0:PW]
                        link(dve.tensor_reduce(m, scores, AX, ALU.max))
                        link(tt(m, m, sink, ALU.max))
                        link(tt(d, sink, m, ALU.subtract))
                        dve.tensor_scalar(m, m, -1.0, None, ALU.mult).then_inc(s["sw_m"], 1)
                    for e in range(2):
                        n = 2 * (p - SWA0) + e
                        k0 = 0 if n % 4 else P
                        dve.wait_ge(s["sw_e"], n + 1)
                        link(tt(srin[:, e], ssum[:, e], sd[:, e], ALU.add))
                        link(dve.reciprocal(srin[:, e], srin[:, e]))
                        tt(sE[:, e, :, k0:PW], sE[:, e, :, k0:PW], srin[:, e].unsqueeze(2).to_broadcast([P, 4, PW - k0]), ALU.mult)\
                            .then_inc(s["sw_n"], 1)
                if DIFF0 <= p < DIFF0 + 16:
                    for e in range(2):
                        n = 2 * (p - DIFF0) + e
                        nk = (n % 4 + 1) * P
                        dve.wait_ge(s["df_s"], n + 1)
                        dve.tensor_reduce(dm[:, e], PS[:, 4 + 2 * e:6 + 2 * e, 0:nk], AX, ALU.max, negate=True).then_inc(s["df_m"], 1)
                    for e in range(2):
                        n = 2 * (p - DIFF0) + e
                        nk = (n % 4 + 1) * P
                        dve.wait_ge(s["df_e"], n + 1)
                        link(dve.reciprocal(drin[:, e], dsum[:, e]))
                        link(tt(drin[:, e, 1:2], drin[:, e, 1:2], nlam, ALU.mult))
                        if n >= 2:
                            dve.wait_ge(s["df_T"], n - 1)
                        link(dve.tensor_scalar(dA[:, e, 0:nk], dE[:, e, 0, 0:nk], drin[:, e, 0:1], None, ALU.mult))
                        stt(dA[:, e, 0:nk], dE[:, e, 1, 0:nk], drin[:, e, 1:2], dA[:, e, 0:nk], ALU.mult, ALU.add).then_inc(s["df_a"], 1)
                if p in DIFF_END:
                    h2 = DIFF_END[p]
                    dve.wait_ge(s["df_sq"], h2 + 1)
                    link(dve.reciprocal(drs, dss))
                    tt(dO, dO, drs.unsqueeze(2).to_broadcast([P, 8, P]), ALU.mult).then_inc(s["df_n"], 1)

            def between(p):
                if p in SSD_SLOT:
                    q = SSD_SLOT.index(p)
                    g, c = divmod(q, 4)
                    yf = yt.rearrange("p j n -> p (j n)")
                    dve.wait_ge(s["ssd_out"], q + 1)
                    if c == 0:
                        dve.tensor_copy(state.rearrange("p j n -> p (j n)"), PS[:, 5, :]).then_inc(s["ssd_st"], 1)
                    elif c < 3:
                        link(tt(state, state, cdec[:, c, 8 * g:8 * g + 8].unsqueeze(2).to_broadcast([P, 8, HD]), ALU.mult))
                        tt(state.rearrange("p j n -> p (j n)"), state.rearrange("p j n -> p (j n)"), PS[:, 5, :], ALU.add)\
                            .then_inc(s["ssd_st"], 1)
                    link(tt(yf, yf, PS[:, 4, :], ALU.add))
                    if c > 0:
                        link(tt(inter, PS[:, 7, :].rearrange("p (j n) -> p j n", j=8),
                                ecs[:, c, 8 * g:8 * g + 8].unsqueeze(2).to_broadcast([P, 8, HD]), ALU.mult))
                        link(tt(yf, yf, inter.rearrange("p j n -> p (j n)"), ALU.add))
                    tt(z[g][:, c, :], z[g][:, c, :], yf, ALU.mult).then_inc(s["ssd_y"], 1)
                if p in SSD_END:
                    g = SSD_END[p]
                    for t in range(4):
                        f = 4 * g + t
                        dve.wait_ge(s["yb_hi"], f + 1)
                        stt(Y_LO[1][:, f, :], PS[:, 4 + t, :], colB[:, B_NG + f:B_NG + f + 1], Y_HI[1][:, f, :], ALU.mult, ALU.subtract)\
                            .then_inc(s["yb_lo"], 1)
                if SWA0 <= p < SWA0 + 8:
                    for e in range(2):
                        n = 2 * (p - SWA0) + e
                        k0 = 0 if n % 4 else P
                        dve.wait_ge(s["sw_T"], n + 1)
                        if n >= 2:
                            dve.wait_ge(s["sw_o"], n - 1)
                        dve.tensor_copy(sPT[:, e, 0:2, k0:PW], PS[:, 4 + 2 * e, :].rearrange("p (k n) -> p k n", k=2)[:, :, k0:PW])\
                            .then_inc(s["sw_Tv"], 1)

            def after(p):
                if p + 1 in SSD_SLOT:
                    ssd_triangle(SSD_SLOT.index(p + 1))
                if SWA0 <= p < SWA0 + 8:
                    for e in range(2):
                        n = 2 * (p - SWA0) + e
                        j, i = divmod(n, 4)
                        dve.wait_ge(s["sw_o"], n + 1)
                        if n >= 2:
                            dve.wait_ge(s["y_lo"], 8 + n - 1)
                        stt(sy[:, e], PS[:, 4 + 2 * e, 0:PW].rearrange("p (u n) -> p u n", u=2), 1.0 / P,
                            gC[j % 2][:, :, i * P:i * P + P], ALU.mult, ALU.mult).then_inc(s["sw_y"], 1)
                if p in DIFF_END:
                    h2 = DIFF_END[p]
                    for u in range(2):
                        dve.wait_ge(s["df_nT"], 2 * h2 + u + 1)
                        if h2 > 0:
                            dve.wait_ge(s["y_lo"], 24 + 2 * h2 - 1 + u)
                        stt(dy[:, u, :], PS[:, 4 + 2 * u, :], ng2, gD[h2 % 2][:, u, :], ALU.mult, ALU.mult).then_inc(s["df_y"], 1)
                if PANELS[p][0] == "br" and PANELS[p][1] >= 12:
                    i = PANELS[p][1] - 12
                    for u in range(2):
                        dve.wait_ge(s["m_hi"], 2 * i + u + 1)
                        stt(Y_LO[0][:, 2 * i + u, :], M[:, 2 * i + u, :], 1.0 / P, Y_HI[0][:, 2 * i + u, :], ALU.mult, ALU.subtract)\
                            .then_inc(s["m_lo"], 1)

            dve.wait_ge(s["ss_ready"], 1)
            link(dve.reciprocal(rin, ss))
            for q in range(ST):
                dve.tensor_scalar(Mseq[:, q, :], xres[:, q, :], rin[:, q:q + 1], None, ALU.mult).then_inc(s["xn_ready"], 1)
            dve.wait_ge(s["cols_ready"], 2)
            link(dve.tensor_scalar(halfA[:, :], colA[:, :], 0.5, None, ALU.mult))
            for k in range(KT):
                dve.wait_ge(s["h_hi"], k + 1)
                stt(hT[:, 1, k, :], PS[:, k, :], colA[:, A_G + k:A_G + k + 1], hT[:, 0, k, :], ALU.mult, ALU.subtract)\
                    .then_inc(s["h_lo"], 1)
            dve.wait_ge(s["dtw_hi"], 1)
            stt(dtws[:, 1].rearrange("p k n -> p (k n)"), dtw.rearrange("p k n -> p (k n)"), WS,
                dtws[:, 0].rearrange("p k n -> p (k n)"), ALU.mult, ALU.subtract).then_inc(s["dtw_lo"], 1)
            split_lo(0)
            for p in range(NP):
                if p + 1 < NP:
                    split_lo(p + 1)
                before(p)
                between(p)
                evacuate(p)
                after(p)
            dve.wait_ge(s["fin_ss"], 1)
            dve.wait_ge(s["post_in"], 16)
            link(dve.reciprocal(rin, ss))
            for q in range(ST):
                link(stt(Mseq[:, q, :], Mseq[:, q, :], rin[:, q:q + 1], pg, ALU.mult, ALU.mult))
                link(tt(xres[:, q, :], xres[:, q, :], Mseq[:, q, :], ALU.add))

        @block.gpsimd
        def _(pool):
            def tt(o, a, b, op):
                return pool.tensor_tensor(o, a, b, op)

            def rope(p):
                n = rope_index(p)
                pool.wait_ge(s["rope_dma"], 64 * (n + 1))
                tt(rswap, rswap, sinT.unsqueeze(1).to_broadcast([P, 2, S]), ALU.mult).then_inc(s["rope_sin"], 1)

            pool.memset(wbd.rearrange("p t r n -> p (t r n)"), 0.0).then_inc(s["wbd_zero"], 1)
            for p in range(NP):
                if p > 0 and PANELS[p - 1][0] == "ga":
                    j = PANELS[p - 1][1]
                    for u in range(2):
                        t = 2 * j + u
                        pool.wait_ge(s["lru_a"], t + 1)
                        pool.wait_ge(s["lru_v"], t + 1)
                        tt(rbuf[:, u, :], abuf[:, u, :], abuf[:, u, :], ALU.mult).then_inc(s["lru_a2"], 1)
                    pool.wait_ge(s["lru_beta"], j + 1)
                    for u in range(2):
                        t = 2 * j + u
                        pool.wait_ge(s["lru_ww"], t + 1)
                        tt(wbuf[:, u, :], wbuf[:, u, :], vbuf[:, u, :], ALU.mult).then_inc(s["lru_bw"], 1)
                    for u in range(2):
                        t = 2 * j + u
                        pool.wait_ge(s["y_hi"], t + 1)
                        tt(Y_LO[0][:, t, :], hbuf[:, u, :], Y_HI[0][:, t, :], ALU.subtract).then_inc(s["y_lo"], 1)
                if p in SSD_SLOT:
                    q = SSD_SLOT.index(p)
                    g, c = divmod(q, 4)
                    if q > 0:
                        pool.wait_ge(s["ssd_out"], q)
                        pool.wait_ge(s["ssd_y"], q)
                    if c == 0:
                        pool.wait_ge(s["xt_read"], 6 + 4 * g)
                        pool.wait_ge(s["dec_ready"], 1)
                        pool.wait_ge(s["dta_ready"], 1)
                    xv = xs[g][:, c, :].rearrange("p (j n) -> p j n", j=8)

                    def head(v):
                        return v.unsqueeze(2).to_broadcast([P, 8, HD])
                    hs = slice(8 * g, 8 * g + 8)
                    tt(xdt, xv, head(dtv[:, c, hs]), ALU.mult).then_inc(s["pool_chain"], 1)
                    tt(yt, xv, head(rowp[:, R_D + 8 * g:R_D + 8 * g + 8]), ALU.mult)
                    pool.wait_ge(s["pool_chain"], q + 1)
                    tt(xw, xdt, head(dend[:, c, hs]), ALU.mult).then_inc(s["ssd_x"], 1)
                if PANELS[p][0] in ("kc", "qc", "qd", "kd"):
                    rope(p)
                if SWA0 <= p < SWA0 + 8:
                    for e in range(2):
                        n = 2 * (p - SWA0) + e
                        j, i = divmod(n, 4)
                        pool.wait_ge(s["y_hi"], 8 + n + 1)
                        tt(Y_LO[0][:, 2 * j:2 * j + 2, i * P:i * P + P], sy[:, e], Y_HI[0][:, 2 * j:2 * j + 2, i * P:i * P + P],
                           ALU.subtract).then_inc(s["y_lo"], 1)
                if p in DIFF_END:
                    h2 = DIFF_END[p]
                    for u in range(2):
                        pool.wait_ge(s["y_hi"], 24 + 2 * h2 + u + 1)
                        tt(Y_LO[1][:, 2 * h2 + u, :], dy[:, u, :], Y_HI[1][:, 2 * h2 + u, :], ALU.subtract).then_inc(s["y_lo"], 1)
                if PANELS[p][0] == "br" and PANELS[p][1] >= 4:
                    i = PANELS[p][1]
                    for u in range(2):
                        pool.wait_ge(s["dve_free"], dve_frees(2 * p + u))
                        t = 2 * (i % 4) + u
                        tt(M[:, t, :], M[:, t, :], T[:, S * u:S * u + S], ALU.add).then_inc(s["m_acc"], 1)

        block_guard.__exit__(None, None, None)
        for n in names:
            if n not in ("consts_in", "x_in", "stored"):
                nc.gpsimd.sem_clear(s[n])
        nc.all_engine_barrier()
        layer_loop.__exit__(None, None, None)

        with nc.Block() as block:
            @block.sync
            def _(sp):
                sp.dma_start(out.rearrange("b (s p) n -> p (b s) n", p=P), xres[:, :, :]).then_inc(s["stored"], 16)
                sp.wait_ge(s["stored"], 16)


def rope_index(p):
    return sum(PANELS[q][0] in ("kc", "qc", "qd", "kd") for q in range(p))


def shape_constants():
    k = np.zeros((P, K_N), np.float32)
    i = np.arange(P)
    k[:, K_ID:K_ID + P] = np.eye(P)
    k[:, K_TRI:K_TRI + P] = i[:, None] <= i[None, :]
    k[:, K_STRICT:K_STRICT + P] = i[:, None] > i[None, :]
    k[:, K_ONES:K_ONES + P] = 1
    inv = (1.0 / (np.float32(10000.0) ** (np.arange(0, HD, 2, dtype=np.float32) / HD))).astype(np.float32)
    ang = (np.arange(S, dtype=np.float32)[None, :] * inv[i % 32][:, None]).astype(np.float32)
    k[:, K_COS:K_COS + S] = np.cos(ang)
    k[:, K_SIN:K_SIN + S] = np.sin(ang) * np.where(i % HD < 32, -1, 1)[:, None]
    for b in (0, HD):
        k[b, K_ML:K_ML + HD] = 1
        k[b + 1, K_ML + HD:K_ML + P] = 1
        k[b, K_MR:K_MR + HD] = NEG
        k[b, K_MR + 192:K_MR + 256] = NEG
        k[b + 1, K_MR:K_MR + P] = NEG
    return k


def kernel(**inputs):
    import concourse.bacc as bacc
    from concourse.bass_utils import run_bass_kernel_spmd

    a = {n: np.ascontiguousarray(v) for n, v in inputs.items()}
    tiles = lambda v: v.reshape(L, -1, P)
    li = np.array([[0.8 - 0.6 * math.exp(-0.3 * l)] for l in range(L)])
    arrays = {
        "x": a["x"], "w_in": a["w_in"], "w_branch": a["w_branch"].reshape(L * 4, D, D), "w_out": a["w_out"],
        "w_r": a["lru_w_r"], "w_i": a["lru_w_i"],
        "cols_a": np.concatenate([tiles(a[n]) for n in ("pre_norm_g", "b_merge", "lru_conv_w", "lru_conv_b", "lru_b_r",
                                                         "lru_b_i", "lru_lambda")], axis=1),
        "cols_b": np.concatenate([tiles(a[n]) for n in ("ssd_conv_w", "ssd_conv_b", "ssd_norm_g", "diff_norm_g")], axis=1),
        "rows": np.concatenate([a[n] for n in ("ssd_dt_bias", "ssd_a_log", "ssd_d", "swa_sinks", "diff_lq1", "diff_lk1",
                                               "diff_lq2", "diff_lk2")]
                               + [li.astype(np.float32), (1 - li).astype(np.float32)], axis=1).reshape(L, 1, R_N),
        "post_g": a["post_norm_g"].reshape(L, 1, D),
        "consts": shape_constants(),
    }
    nc = bacc.Bacc("TRN2", target_bir_lowering=False, num_devices=1)
    aps = [nc.dram_tensor(n, v.shape, F32, kind="ExternalInput").ap() for n, v in arrays.items()]
    res = nc.dram_tensor("out", (1, S, D), F32, kind="ExternalOutput").ap()
    program(nc, *aps, res)
    r = run_bass_kernel_spmd(nc, [arrays], core_ids=[0])
    return r.results[0]["out"]
```

```python
import math
from contextlib import ExitStack

import numpy as np

import concourse.bass as bass
from concourse import mybir

F32 = mybir.dt.float32
F16 = mybir.dt.float16
BF16 = mybir.dt.bfloat16
ACT = mybir.ActivationFunctionType
ALU = mybir.AluOpType
AX = mybir.AxisListType.X

P = 128
D = 1024
S = 512
L = 2
KT = D // P
ST = S // P
HD = 64
PW = 256
EPS = 1e-6
WS = 64.0
IWS = 1.0 / WS
NS = 2
NB = 2
NEG = -1e30

C_XA, C_GA, C_Z, C_XBC = 0, D, 2 * D, 3 * D
C_DT = C_XBC + D + 512
C_QC = C_DT + 16
C_KC, C_VC, C_GC = C_QC + D, C_QC + D + 256, C_QC + D + 512
C_QD = C_GC + D
C_KD, C_VD, C_GD, C_MG = C_QD + D, C_QD + 2 * D, C_QD + 3 * D, C_QD + 4 * D

PANELS = []
for _j in range(4):
    PANELS += [("xa", _j, "in", C_XA + PW * _j), ("ga", _j, "in", C_GA + PW * _j)]
PANELS += [("conv", 8, "in", C_XBC + D), ("conv", 10, "in", C_XBC + D + PW),
           ("kc", 0, "in", C_KC), ("vc", 0, "in", C_VC)]
for _g in range(2):
    PANELS += [("conv", 4 * _g, "in", C_XBC + 2 * _g * PW), ("conv", 4 * _g + 2, "in", C_XBC + (2 * _g + 1) * PW),
               ("z", 2 * _g, "in", C_Z + 2 * _g * PW), ("z", 2 * _g + 1, "in", C_Z + (2 * _g + 1) * PW)]


def _merge(n):
    out = []
    for c in range(4):
        out += [("mg", 4 * n + c, "in", C_MG + n * D + PW * c), ("br", 4 * n + c, "br", PW * c)]
    return out


PANELS += _merge(0)
for _j in range(4):
    PANELS += [("qc", _j, "in", C_QC + PW * _j), ("gc", _j, "in", C_GC + PW * _j)]
PANELS += _merge(1)
for _j in range(4):
    PANELS += [("qd", _j, "in", C_QD + PW * _j), ("vd", _j, "in", C_VD + PW * _j),
               ("kd", _j, "in", C_KD + PW * _j), ("gd", _j, "in", C_GD + PW * _j)]
PANELS += _merge(2) + _merge(3)
PANELS += [("out", c, "out", PW * c) for c in range(4)]
NP = len(PANELS)
SLOT = {(k, i): p for p, (k, i, _, _) in enumerate(PANELS)}

VECTOR_FREES = {"ga", "z", "gc", "gd", "br"}
ROTATED = ("kc", "qc", "qd", "kd")
SSD_SLOT = [16, 17, 18, 19, 21, 22, 23, 24]
SSD_END = {20: 0, 25: 1}
SWA0 = SLOT[("qc", 0)] + 3
DIFF0 = SLOT[("qd", 0)] + 5
DIFF_END = {DIFF0 + 4 * h + 4: h for h in range(4)}
CONV_SLOTS = [p for p in range(NP) if PANELS[p][0] in ("xa", "conv")]


def product_steps(p):
    if DIFF0 <= p < DIFF0 + 16 or SWA0 <= p < SWA0 + 8:
        return 10, 13
    if p in SSD_SLOT:
        return 8, 12
    if p in SSD_END:
        return 8, 14
    if p == SLOT[("conv", 10)]:
        return 8, 15
    return 8, 12


def freed_by_vector(tile):
    return PANELS[tile // 2][0] in VECTOR_FREES


def act_frees(tile):
    return sum(not freed_by_vector(t) for t in range(tile + 1))


def dve_frees(tile):
    return sum(freed_by_vector(t) for t in range(tile + 1))


def transposed_before(p):
    return sum(2 for q in range(p - 1) if PANELS[q][0] == "conv" and PANELS[q][1] != 10)


def gate_writes(tile):
    return sum(PANELS[t // 2][0] in ("ga", "z", "gc", "gd", "mg") for t in range(tile))


def gate_uses(tile):
    return sum(PANELS[t // 2][0] in ("ga", "z", "gc", "gd") for t in range(tile + 1))


def conv_tiles(p):
    return 2 * sum(q < p for q in CONV_SLOTS)


K_ID, K_TRI, K_ONES, K_COS, K_SIN = 0, 128, 256, 384, 896
K_KEPT = 1408
K_STRICT, K_ML, K_MR, K_N = 1408, 1536, 1664, 1920
A_G, A_BM, A_CW, A_CB, A_BR, A_BI, A_LAM, A_N = 0, 8, 40, 72, 80, 88, 96, 104
B_CW, B_CB, B_NG, B_DG, B_N = 0, 48, 60, 68, 69
R_DTB, R_AL, R_D, R_SINK, R_LQ, R_LI, R_N = 0, 16, 32, 48, 64, 320, 322


def program(nc, x, w_in, w_branch, w_out, w_r, w_i, cols_a, cols_b, rows, post_g, consts, out):
    ctx = ExitStack()
    with ctx:
        def sb(name, shape, dt=F32):
            return ctx.enter_context(nc.sbuf_tensor(name, shape, dt))

        xres = sb("xres", [P, ST, D])
        hT = sb("hT", [P, 2, KT, S], F16)
        M = sb("M", [P, 8, S])
        ys = sb("ys", [P, 2, 4096])
        X = sb("X", [P, 11264])
        Y = sb("Y", [P, 8416])
        stage = sb("stage", [P, NS, KT, PW])
        wsp = sb("wsp", [P, NB, 2, KT, PW], F16)
        G = sb("G", [P, 2, S])
        T = sb("T", [P, 1032])
        K = sb("K", [P, K_KEPT])
        rowp = sb("rowp", [P, R_N])
        colA = sb("colA", [P, A_N])
        halfA = sb("halfA", [P, A_N])
        masks = sb("masks", [P, 3 * P], BF16)
        tris = sb("tris", [P, 2 * P], F16)
        colB = sb("colB", [P, B_N])
        small = sb("small", [P, 104])
        PS = ctx.enter_context(nc.psum_tensor("PS", [P, 8, 512], F32))

        ident, tri, ones = (K[:, a:a + P] for a in (K_ID, K_TRI, K_ONES))
        maskQ, maskK = masks[:, 0:P], masks[:, P:3 * P]
        strict16, tri16 = tris[:, 0:P], tris[:, P:2 * P]
        cosT, sinT = K[:, K_COS:K_COS + S], K[:, K_SIN:K_SIN + S]

        def half(b, part):
            return ys[:, b, 2048 * part:2048 * part + 2048].bitcast(F16).rearrange("p (t s) -> p t s", s=S)

        Y_HI = [half(0, 0), half(1, 0)]
        Y_LO = [half(0, 1), half(1, 1)]

        xpad = T[:, 0:1032].rearrange("p (u s) -> p u s", u=2)
        cbuf, rbuf, wbuf, abuf = (M[:, 2 * i:2 * i + 2, :] for i in range(4))
        lru_mem = ys[:, 1, :].rearrange("p (t s) -> p t s", s=S)
        vbuf, gbuf, hbuf = (lru_mem[:, 2 * i:2 * i + 2, :] for i in range(3))
        BT = X[:, 0:1024].rearrange("p (g s) -> p g s", g=2)
        CT = X[:, 1024:2048].rearrange("p (g s) -> p g s", g=2)
        Bseq = X[:, 2048:3072].rearrange("p (c n) -> p c n", c=ST)
        xs = [X[:, 3072 + 4096 * g:5120 + 4096 * g].rearrange("p (c n) -> p c n", c=ST) for g in range(2)]
        z = [X[:, 5120 + 4096 * g:7168 + 4096 * g].rearrange("p (c n) -> p c n", c=ST) for g in range(2)]
        sE = X[:, 0:2048].rearrange("p (e k n) -> p e k n", e=2, k=4)
        sPT = X[:, 2048:4096].rearrange("p (e k n) -> p e k n", e=2, k=4)
        sy = X[:, 4096:4608].rearrange("p (e u n) -> p e u n", e=2, u=2)
        def pair(at):
            return [X[:, at + 1024 * b:at + 1024 * b + 1024].rearrange("p (u s) -> p u s", u=2) for b in range(2)]
        gD = pair(4096)
        def stacked(v):
            return v.bitcast(F16).rearrange("p (t u s) -> p t u s", t=2, u=2)
        qD = [stacked(X[:, 1024 * b:1024 * b + 1024]) for b in range(2)]
        kD = [stacked(X[:, 2048 + 1024 * b:3072 + 1024 * b]) for b in range(2)]
        kloD = [Y[:, 7168 + 512 * b:7680 + 512 * b].bitcast(F16).rearrange("p (u s) -> p u s", u=2) for b in range(2)]
        rlo = T[:, 0:512].bitcast(F16).rearrange("p (u s) -> p u s", u=2)
        vD = [X[:, 6144 + 1024 * b:7168 + 1024 * b].rearrange("p (c n) -> p c n", c=ST) for b in range(2)]
        rraw, rswap, rcos = (X[:, 8192 + 1024 * b:9216 + 1024 * b].rearrange("p (u s) -> p u s", u=2) for b in range(3))
        kC, kloC = stacked(Y[:, 0:1024]), stacked(Y[:, 1024:2048])
        vC = Y[:, 2048:3072].rearrange("p (c n) -> p c n", c=ST)
        qC = [stacked(Y[:, 3072 + 1024 * b:4096 + 1024 * b]) for b in range(2)]
        gC = [Y[:, 5120 + 1024 * b:6144 + 1024 * b].rearrange("p (u s) -> p u s", u=2) for b in range(2)]
        wbd = Y[:, 3072:5120].rearrange("p (t r n) -> p t r n", t=8, r=2)
        dtw = Y[:, 2048:2176].rearrange("p (k n) -> p k n", k=KT)
        dtws = Y[:, 2176:2304].bitcast(F16).rearrange("p (h k n) -> p h k n", h=2, k=KT)
        dtri = Y[:, 3072:4096].bitcast(F16).rearrange("p (h j l) -> p h j l", h=2, j=8)
        est = Y[:, 4096:5120].rearrange("p (j l) -> p j l", j=8)
        xdt, xw, state, yt = (Y[:, 5120 + 512 * i:5632 + 512 * i].rearrange("p (j n) -> p j n", j=8) for i in range(4))
        gm = Y[:, 7168:7296]
        dtv, dta, cs, ecs, dend, cdec = (Y[:, 7296 + 64 * i:7360 + 64 * i].rearrange("p (c j) -> p c j", c=ST) for i in range(6))
        spw = Y[:, 7680:8400].rearrange("p (i n) -> p i n", n=72)
        ea = Y[:, 8400:8416]
        inter = Y[:, 7680:8192].rearrange("p (j n) -> p j n", j=8)
        dta16 = cs.rearrange("p c j -> p (c j)").bitcast(F16).rearrange("p (h c j) -> p h c j", h=2, c=ST)
        dE = Y[:, 0:2048].rearrange("p (e t n) -> p e t n", e=2, t=2)
        dA = Y[:, 2048:3072].rearrange("p (e n) -> p e n", e=2)
        dPT = Y[:, 3072:4096].rearrange("p (e n) -> p e n", e=2)
        dO = Y[:, 4096:5120].rearrange("p (n e) -> p n e", n=8)
        dy = Y[:, 5120:6144].rearrange("p (u s) -> p u s", u=2)
        dsq = Y[:, 6144:7168].rearrange("p (n e) -> p n e", n=8)
        pg = Y[:, 0:1024]
        Mseq = M[:, :, :].rearrange("p a b -> p (a b)").rearrange("p (s n) -> p s n", s=ST)
        rowsA, rowsB = X[0:A_N, 0:P], X[0:B_N, P:2 * P]
        ss, rin = small[:, 0:4], small[:, 88:92]
        sm = small[:, 8:16].rearrange("p (e k) -> p e k", e=2)
        sd = small[:, 16:24].rearrange("p (e k) -> p e k", e=2)
        ssum = small[:, 24:32].rearrange("p (e k) -> p e k", e=2)
        srin = small[:, 32:40].rearrange("p (e k) -> p e k", e=2)
        dm = small[:, 40:44].rearrange("p (e t) -> p e t", e=2)
        dsum = small[:, 44:48].rearrange("p (e t) -> p e t", e=2)
        drin = small[:, 48:52].rearrange("p (e t) -> p e t", e=2)
        dss, drs = small[:, 52:60], small[:, 60:68]
        eps = small[:, 68:69]
        nlam, ng2 = small[:, 69:70], small[:, 70:71]
        sp4, nsp4 = small[:, 72:80], small[:, 80:88]
        lsum = small[:, 102:104]
        part = small[:, 8:24].rearrange("p (q c) -> p q c", q=ST)
        nss = small[:, 4:8]
        gss, grin = small[:, 92:96], small[:, 96:100]

        kept = ["consts_in", "x_in", "stored", "first_in", "first_ss"]
        names = ["next_in", "wbd_zero", "wbd_in", "post_in",
                 "load0", "load1", "hi_done", "lo_done", "panel_done", "tile_done", "act_free", "dve_free", "gate_ready",
                 "act_chain", "dve_chain", "pool_chain",
                 "ss_ready", "rin_ready", "xn_ready", "cols_T", "cols_ready", "xn_T", "h_hi", "h_lo",
                 "dtw_hi", "dtw_lo", "dt_raw", "sp_in", "sp_exp", "dta_ready", "cs_done", "cs_ready", "dec_ready", "lru_par",
                 "conv_done", "lru_gates", "lru_a", "lru_v", "lru_w", "lru_a2", "lru_vv", "lru_ww", "lru_beta", "lru_bw",
                 "lru_y", "y_hi", "y_lo", "conv_tanh", "conv_silu", "xt_done", "xt_read",
                 "rope_dma", "rope_sin", "rope_done", "rope_hi", "rope_lo", "rope_stack",
                 "ssd_tri", "ssd_x", "ssd_g", "ssd_exp", "ssd_mt", "ssd_y", "ssd_out", "ssd_st", "ssd_ss", "ssd_norm", "ssd_T",
                 "yb_hi", "yb_lo", "sw_zero", "sw_s", "sw_m", "sw_e", "sw_n", "sw_T", "sw_Ta", "sw_Tv", "sw_o", "sw_y",
                 "lam_e", "df_s", "df_m", "df_e", "df_a", "df_T", "df_Tr", "df_o", "df_or", "df_ss", "df_sq", "df_n", "df_nT", "df_y",
                 "m_acc", "m_hi", "m_lo", "fin_ss", "fin_sum", "fin_y", "x_pool", "x_dve", "dta16_ready"]
        s = {n: ctx.enter_context(nc.semaphore(n)) for n in kept + names}
        load = [s["load0"], s["load1"]]

        def panel_source(p, of_layer):
            kind, i, which, c0 = PANELS[p]
            if which == "in":
                src = w_in[bass.ds(of_layer, 1), :, c0:c0 + PW]
            elif which == "br":
                src = w_branch[bass.ds(of_layer * 4 + i // 4, 1), :, c0:c0 + PW]
            else:
                src = w_out[bass.ds(of_layer, 1), :, c0:c0 + PW]
            return src.rearrange("a (k p) n -> p (a k) n", p=P)

        def load_first(sp, of_layer, landed):
            sp.dma_start(rowsA, cols_a[bass.ds(of_layer, 1)].rearrange("a r p -> (a r) p")).then_inc(landed, 16)
            sp.dma_start(rowsB, cols_b[bass.ds(of_layer, 1)].rearrange("a r p -> (a r) p")).then_inc(landed, 16)
            sp.dma_start(stage[:, 0], panel_source(0, of_layer)).then_inc(landed, 16)
            sp.dma_start(dtw, w_in[bass.ds(of_layer, 1), :, C_DT:C_DT + 16].rearrange("a (k p) n -> p (a k) n", p=P))\
                .then_inc(landed, 16)
            sp.dma_start(rowp[:, :], rows[bass.ds(of_layer, 1)].rearrange("a b n -> (a b) n").to_broadcast([P, R_N]))\
                .then_inc(landed, 16)
            sp.dma_start(stage[:, 1], panel_source(1, of_layer)).then_inc(landed, 16)

        with nc.Block() as block:
            @block.sync
            def _(sp):
                for q in range(ST):
                    sp.dma_start(xres[:, q, :], x[0, q * P:q * P + P, :]).then_inc(s["x_in"], 16)
                sp.dma_start(K[:, :], consts[:, 0:K_KEPT]).then_inc(s["consts_in"], 16)
                sp.dma_start(Y[:, 0:K_N - K_KEPT], consts[:, K_KEPT:K_N]).then_inc(s["consts_in"], 16)
                load_first(sp, 0, s["first_in"])
                sp.wait_ge(s["first_in"], 96)
                sp.wait_ge(s["consts_in"], 32)
                sp.wait_ge(s["x_in"], 64)

            @block.scalar
            def _(act):
                act.wait_ge(s["x_in"], 64)
                for q in range(ST):
                    act.activation(M[:, 2 * q:2 * q + 2, :].rearrange("p a b -> p (a b)"), xres[:, q, :], ACT.Square,
                                   accum_out=nss[:, q:q + 1])

            @block.vector
            def _(dve):
                dve.memset(eps, EPS)
                dve.wait_ge(s["consts_in"], 32)
                dve.tensor_copy(strict16, Y[:, 0:P])
                dve.tensor_copy(masks[:, :], Y[:, P:4 * P])
                dve.tensor_copy(tri16, tri)

        layer_loop = nc.Fori(0, L)
        layer = layer_loop.__enter__()
        block_guard = nc.Block()
        block = block_guard.__enter__()

        @block.sync
        def _(sp):
            def load_panel(p):
                sp.wait_ge(s["lo_done"], p - NS + 1)
                sp.dma_start(stage[:, p % NS], panel_source(p, layer)).then_inc(load[p % NS], 16)

            sp.wait_ge(s["wbd_zero"], 1)
            for r, w in enumerate((w_r, w_i)):
                for o in range(2):
                    sp.dma_start(wbd[HD * o:HD * o + HD, :, r, HD * o:HD * o + HD],
                                 w[bass.ds(layer, 1)].rearrange("a (t o) i j -> o i (a t) j", o=2)[o])\
                        .then_inc(s["wbd_in"], 16)
            for p in range(2, NP):
                load_panel(p)
                if p >= 4 and PANELS[p - 4][0] in ROTATED:
                    kind, i = PANELS[p - 4][0:2]
                    sp.wait_ge(s["rope_hi"], 2 * rope_index(p - 4) + 2)
                    sp.wait_ge(s["rope_lo"], 2 * rope_index(p - 4) + 2)
                    for t, (own, other) in enumerate(((slice(0, HD), slice(HD, P)), (slice(HD, P), slice(0, HD)))):
                        if kind == "kc":
                            moves = ((kC[other, t], kC[own, t]), (kloC[other, t], kloC[own, t]))
                        elif kind == "kd":
                            moves = ((kD[i % 2][other, t], kD[i % 2][own, t]),)
                        else:
                            moves = (((qC if kind == "qc" else qD)[i % 2][other, t], rlo[own]),)
                        for o, a in moves:
                            sp.dma_start(o, a).then_inc(s["rope_stack"], 16)
                if PANELS[p - 2][0] in ROTATED:
                    sp.wait_ge(s["act_free"], act_frees(2 * (p - 2) + 1))
                    if rope_index(p - 2) > 0:
                        sp.wait_ge(s["rope_done"], rope_index(p - 2))
                    for a, b in ((0, 32), (32, 0), (64, 96), (96, 64)):
                        sp.dma_start(rswap[a:a + 32], rraw[b:b + 32]).then_inc(s["rope_dma"], 16)
            sp.wait_ge(s["y_lo"], 32)
            sp.dma_start(pg, post_g[bass.ds(layer, 1)].rearrange("a b n -> (a b) n").to_broadcast([P, D]))\
                .then_inc(s["post_in"], 16)
            sp.wait_ge(s["lo_done"], NP)
            load_first(sp, layer * -1 + 1, s["next_in"])
            sp.wait_ge(s["next_in"], 96)

        @block.tensor
        def _(pe):
            def mm(o, a, b, start, stop):
                return pe.matmul(o, a, b, start=start, stop=stop, skip_group_check=True)

            def wait_bank(tile):
                if tile >= 4:
                    if freed_by_vector(tile - 4):
                        pe.wait_ge(s["dve_free"], dve_frees(tile - 4))
                    else:
                        pe.wait_ge(s["act_free"], act_frees(tile - 4))

            def operand(p):
                kind, i, which, _ = PANELS[p]
                if which == "in":
                    return hT[:, 0], hT[:, 1]
                if which == "br":
                    n = i // 4
                    if n == 1:
                        pe.wait_ge(s["yb_hi"], 8)
                        pe.wait_ge(s["yb_lo"], 8)
                    else:
                        pe.wait_ge(s["y_lo"], {0: 8, 2: 24, 3: 32}[n])
                    return Y_HI[n % 2], Y_LO[n % 2]
                pe.wait_ge(s["m_lo"], 8)
                return Y_HI[0], Y_LO[0]

            def beside(p, step):
                between_at, middle_at = product_steps(p)
                if step == between_at:
                    between(p)
                if step == middle_at:
                    middle(p)

            def tile_product(p, u):
                b = p % NB
                tile = 2 * p + u
                hi, lo = operand(p)
                if u == 0:
                    pe.wait_ge(s["lo_done"], p + 1)
                    pe.wait_ge(s["hi_done"], p + 1)
                wait_bank(tile)
                bank = PS[:, tile % 4]
                if PANELS[p][0] in ("z", "vc", "vd", "out"):
                    for h in range(2):
                        q = 2 * u + h
                        o = bank[:, PW * h:PW * h + PW]
                        for k in range(KT):
                            if k % 2 == 0:
                                beside(p, 8 * u + 4 * h + k // 2)
                            a, al = hi[:, k, q * P:q * P + P], lo[:, k, q * P:q * P + P]
                            mm(o, a, wsp[:, b, 0, k, :], k == 0, False)
                            mm(o, a, wsp[:, b, 1, k, :], False, False)
                            last = mm(o, al, wsp[:, b, 0, k, :], False, k == KT - 1)
                else:
                    for k in range(KT):
                        beside(p, 8 * u + k)
                        if p == 0 and u == 0:
                            pe.wait_ge(s["h_hi"], k + 1)
                            pe.wait_ge(s["h_lo"], k + 1)
                        wh, wl = wsp[:, b, 0, k, P * u:P * u + P], wsp[:, b, 1, k, P * u:P * u + P]
                        mm(bank, wh, hi[:, k, :], k == 0, False)
                        mm(bank, wh, lo[:, k, :], False, False)
                        last = mm(bank, wl, hi[:, k, :], False, k == KT - 1)
                last.then_inc(s["tile_done"], 1)

            def before(p):
                if p in SSD_SLOT:
                    q = SSD_SLOT.index(p)
                    g, c = divmod(q, 4)
                    if q == 0:
                        pe.wait_ge(s["conv_silu"], 8)
                        pe.wait_ge(s["y_lo"], 8)
                    if q > 0:
                        pe.wait_ge(s["ssd_y"], q)
                        pe.wait_ge(s["ssd_st"], q - (q > 3))
                    if q == 4:
                        pe.wait_ge(s["yb_hi"], 4)
                        pe.wait_ge(s["yb_lo"], 4)
                    pe.wait_ge(s["xt_read"], transposed_before(p))
                    mm(PS[:, 4, 0:P], BT[:, g, c * P:c * P + P], CT[:, g, c * P:c * P + P], True, True)
                    pe.wait_ge(s["ssd_tri"], 2 * q + 2)
                    for h in range(2):
                        for part16 in range(2):
                            last = mm(PS[:, 5 + h, :], strict16, dtri[:, part16, 4 * h:4 * h + 4, :].rearrange("p j l -> p (j l)"),
                                      part16 == 0, part16 == 1)
                    last.then_inc(s["ssd_g"], 1)
                if SWA0 <= p < SWA0 + 8:
                    for e in range(2):
                        n = 2 * (p - SWA0) + e
                        j, i = divmod(n, 4)
                        if n == 0:
                            pe.wait_ge(s["yb_hi"], 8)
                            pe.wait_ge(s["yb_lo"], 8)
                        if i == 0:
                            pe.wait_ge(s["rope_stack"], stacked_after(1 + j))
                        if n >= 2:
                            pe.wait_ge(s["sw_y"], n - 1)
                        k0 = HD if i else P
                        for r in range(4):
                            at = HD * (r % 2)
                            keys = slice((i - 1) * P + k0, (i + 1) * P)
                            q = qC[j % 2][:, r % 2, r // 2, i * P:i * P + P]
                            o = PS[:, 4 + 2 * e + r % 2, PW * (r // 2) + k0:PW * (r // 2) + PW]
                            mm(o, q, kC[:, j % 2, j // 2, keys], True, False)
                            mm(o, q[at:at + HD], kloC[at:at + HD, j % 2, j // 2, keys], False, False)
                            if i:
                                mm(o[:, 0:HD], maskQ[at:at + HD], maskK[at:at + HD, HD:P], False, True)
                            last = mm(o[:, PW - HD - k0:PW - k0], maskQ[at:at + HD], maskK[at:at + HD, PW - HD:PW], False, True)
                        last.then_inc(s["sw_s"], 1)
                if DIFF0 <= p < DIFF0 + 16:
                    for e in range(2):
                        n = 2 * (p - DIFF0) + e
                        h2, u, i = n // 8, (n // 4) % 2, n % 4
                        if n % 8 == 0:
                            pe.wait_ge(s["rope_stack"], stacked_after(6 + 2 * h2))
                        if n == 0:
                            pe.wait_ge(s["sw_y"], 16)
                        if n >= 2:
                            pe.wait_ge(s["df_or"], n - 1)
                        if n % 8 < 2 and h2 > 1:
                            pe.wait_ge(s["df_y"], 2 * h2 - 2)
                        if n % 8 in (2, 3) and h2 > 0:
                            pe.wait_ge(s["df_y"], 2 * h2)
                        for t in range(2):
                            at = HD * t
                            o = PS[:, 4 + 2 * e + t, 0:(i + 1) * P]
                            q, keys = qD[h2 % 2][:, t, u, i * P:i * P + P], slice(0, (i + 1) * P)
                            mm(o, q, kD[h2 % 2][:, t, u, keys], True, False)
                            mm(o, q[at:at + HD], kloD[h2 % 2][at:at + HD, u, keys], False, False)
                            last = mm(o[:, i * P + HD:i * P + P], maskQ[at:at + HD], maskK[at:at + HD, P + HD:PW], False, True)
                        last.then_inc(s["df_s"], 1)

            def between(p):
                if p == 0:
                    pe.wait_ge(s["dtw_hi"], 1)
                    pe.wait_ge(s["dtw_lo"], 1)
                    for q in range(ST):
                        for k in range(KT):
                            o = PS[:, 4, 16 * q:16 * q + 16]
                            mm(o, hT[:, 0, k, q * P:q * P + P], dtws[:, 0, k, :], k == 0, False)
                            mm(o, hT[:, 0, k, q * P:q * P + P], dtws[:, 1, k, :], False, False)
                            last = mm(o, hT[:, 1, k, q * P:q * P + P], dtws[:, 0, k, :], False, k == KT - 1)
                    last.then_inc(s["dt_raw"], 1)
                if p == 1:
                    pe.wait_ge(s["dta_ready"], 1)
                    d = dta.rearrange("p c j -> p (c j)")
                    mm(PS[:, 5, 0:64], tri, d, True, True)
                    mm(PS[:, 6, 0:64], ones, d, True, True).then_inc(s["cs_done"], 1)
                if p in SSD_SLOT:
                    q = SSD_SLOT.index(p)
                    g, c = divmod(q, 4)
                    pe.wait_ge(s["ssd_mt"], q + 1)
                    pe.wait_ge(s["ssd_x"], q + 1)
                    for j in range(8):
                        mm(PS[:, 4, HD * j:HD * j + HD], est[:, j, :], xdt[:, j, :], True, True)
                    if c > 0:
                        pe.wait_ge(s["ssd_st"], 3 * g + c)
                        last = mm(PS[:, 6, :], CT[:, g, c * P:c * P + P], state.rearrange("p j n -> p (j n)"), True, True)
                    if c < 3:
                        last = mm(PS[:, 5, :], Bseq[:, c, g * P:g * P + P], xw.rearrange("p j n -> p (j n)"), True, True)
                    last.then_inc(s["ssd_out"], 1)
                if SWA0 <= p < SWA0 + 8:
                    for e in range(2):
                        n = 2 * (p - SWA0) + e
                        pe.wait_ge(s["sw_n"], n + 1)
                        if n == 0:
                            pe.wait_ge(s["sw_zero"], 1)
                        for k in range(4):
                            for b in range(0 if n % 4 else 1, 2):
                                last = pe.transpose(PS[:, 4 + 2 * e + k // 2, PW * (k % 2) + P * b:PW * (k % 2) + P * b + P],
                                                    sE[:, e, k, P * b:P * b + P], ident)
                        last.then_inc(s["sw_T"], 1)
                if DIFF0 <= p < DIFF0 + 16:
                    for e in range(2):
                        n = 2 * (p - DIFF0) + e
                        pe.wait_ge(s["df_a"], n + 1)
                        for b in range(n % 4 + 1):
                            last = pe.transpose(PS[:, 4 + 2 * e, P * b:P * b + P], dA[:, e, P * b:P * b + P], ident)
                        last.then_inc(s["df_T"], 1)

            def middle(p):
                if p > 0 and PANELS[p - 1][0] == "conv" and PANELS[p - 1][1] != 10:
                    i = PANELS[p - 1][1]
                    for u in range(2):
                        n = [8, 0, 2, 4, 6].index(i) * 2 + u
                        pe.wait_ge(s["conv_silu"], conv_tiles(p) - 8 - 1 + u)
                        if n == 0:
                            pe.wait_ge(s["y_lo"], 8)
                        if n >= 2:
                            pe.wait_ge(s["xt_read"], n - 1)
                        if p in SSD_SLOT and u == 0:
                            pe.wait_ge(s["ssd_st"], SSD_SLOT.index(p) + 1)
                        src = BT[:, u, :] if i == 8 else wbuf[:, u, :]
                        for q in range(ST):
                            last = pe.transpose(PS[:, 5 + 2 * u, q * P:q * P + P], src[:, q * P:q * P + P], ident)
                        last.then_inc(s["xt_done"], 1)
                if p in SSD_END:
                    g = SSD_END[p]
                    pe.wait_ge(s["ssd_norm"], g + 1)
                    pe.wait_ge(s["ssd_y"], 4 * g + 4)
                    for t in range(4):
                        for c in range(ST):
                            last = pe.transpose(PS[:, 4 + t, c * P:c * P + P], z[g][:, c, t * P:t * P + P], ident)
                        last.then_inc(s["ssd_T"], 1)
                if PANELS[p][0] == "ga":
                    for u in range(2):
                        t = 2 * PANELS[p][1] + u
                        if t == 0:
                            pe.wait_ge(s["wbd_in"], 64)
                            pe.wait_ge(s["dec_ready"], 1)
                        if t >= 2:
                            pe.wait_ge(s["lru_w"], t - 1)
                            pe.wait_ge(s["lru_v"], t - 1)
                        pe.wait_ge(s["conv_done"], t + 1)
                        mm(PS[:, 4 + 2 * u, :], wbd[:, t, 0, :], cbuf[:, u, :], True, True)
                        mm(PS[:, 5 + 2 * u, :], wbd[:, t, 1, :], cbuf[:, u, :], True, True).then_inc(s["lru_gates"], 1)
                if SWA0 <= p < SWA0 + 8:
                    for e in range(2):
                        n = 2 * (p - SWA0) + e
                        j, i = divmod(n, 4)
                        pe.wait_ge(s["sw_Ta"], n + 1)
                        pe.wait_ge(s["sw_Tv"], n + 1)
                        for k in range(4):
                            r = 2 * (k % 2) + k // 2
                            o = PS[HD * (r % 2):HD * (r % 2) + HD, 4 + 2 * e, P * (r // 2):P * (r // 2) + P]
                            if i:
                                mm(o, vC[:, i - 1, HD * j:HD * j + HD], sPT[:, e, k, 0:P], True, False)
                            last = mm(o, vC[:, i, HD * j:HD * j + HD], sPT[:, e, k, P:PW], i == 0, True)
                        last.then_inc(s["sw_o"], 1)
                if p in DIFF_END:
                    h2 = DIFF_END[p]
                    pe.wait_ge(s["df_n"], h2 + 1)
                    for u in range(2):
                        if p < DIFF0 + 16:
                            pe.wait_ge(s["df_Tr"], 2 * (p - DIFF0) + 1 + u)
                        for i in range(4):
                            last = pe.transpose(PS[:, 4 + 2 * u, P * i:P * i + P], dO[:, 4 * u + i, :], ident)
                        last.then_inc(s["df_nT"], 1)
                if DIFF0 <= p < DIFF0 + 16:
                    for e in range(2):
                        n = 2 * (p - DIFF0) + e
                        h2, u, i = n // 8, (n // 4) % 2, n % 4
                        pe.wait_ge(s["df_Tr"], n + 1)
                        for b in range(i + 1):
                            last = mm(PS[:, 5 + 2 * e, 0:P], dPT[:, e, P * b:P * b + P], vD[h2 % 2][:, b, P * u:P * u + P],
                                      b == 0, b == i)
                        last.then_inc(s["df_o"], 1)

            pe.transpose(PS[:, 0, 0:A_N], rowsA, ident[0:A_N, 0:A_N])
            pe.transpose(PS[:, 1, 0:B_N], rowsB, ident[0:B_N, 0:B_N]).then_inc(s["cols_T"], 1)
            pe.wait_ge(s["cols_ready"], 2)
            for k in range(KT):
                for q in range(ST):
                    if k == 0:
                        pe.wait_ge(s["xn_ready"], q + 1)
                    last = pe.transpose(PS[:, k, q * P:q * P + P], Mseq[:, q, k * P:k * P + P], ident)
                last.then_inc(s["xn_T"], 1)
            for p in range(NP):
                before(p)
                tile_product(p, 0)
                tile_product(p, 1)

        @block.scalar
        def _(act):
            chain = [0]

            def link(ins):
                chain[0] += 1
                ins.then_inc(s["act_chain"], 1)
                act.wait_ge(s["act_chain"], chain[0])

            def split_hi(p):
                if p >= NS:
                    act.wait_ge(load[p % NS], 16 * (p // NS))
                if p >= NB:
                    act.wait_ge(s["tile_done"], 2 * (p - NB + 1))
                act.activation(wsp[:, p % NB, 0], stage[:, p % NS], ACT.Copy, scale=WS).then_inc(s["hi_done"], 1)

            def copy(o, i, scale=1.0):
                return act.activation(o, i, ACT.Copy, scale=scale)

            def evacuate(p, u):
                kind, i, _, _ = PANELS[p]
                tile = 2 * p + u
                bank = PS[:, tile % 4]
                act.wait_ge(s["tile_done"], tile + 1)
                if kind in ("ga", "z", "gc", "gd", "mg"):
                    n = gate_writes(tile)
                    if n >= 2:
                        act.wait_ge(s["dve_free"], n - 1)
                    if kind == "mg":
                        bm = halfA[:, A_BM + 2 * i + u:A_BM + 2 * i + u + 1]
                        act.activation(G[:, u], bank, ACT.Tanh, scale=0.5 * IWS, bias=bm).then_inc(s["act_free"], 1)
                    else:
                        act.activation(G[:, u], bank, ACT.Tanh, scale=0.5 * IWS).then_inc(s["gate_ready"], 1)
                elif kind in ("xa", "conv"):
                    n = conv_tiles(p) + u
                    if n >= 2:
                        act.wait_ge(s["conv_done"], n - 1)
                    copy(xpad[:, u, 3:3 + S], bank, IWS).then_inc(s["act_free"], 1)
                elif kind in ROTATED:
                    n = rope_index(p)
                    if n >= 1:
                        act.wait_ge(s["rope_done"], n)
                    if kind == "qd" and i == 0:
                        act.wait_ge(s["y_lo"], 24)
                    copy(rraw[:, u, :], bank, IWS if kind in ("kc", "kd") else IWS / 8).then_inc(s["act_free"], 1)
                elif kind in ("vc", "vd"):
                    if kind == "vd" and i >= 2:
                        act.wait_ge(s["df_o"], 8 * (i - 1))
                    dst = vC if kind == "vc" else vD[i % 2]
                    copy(dst[:, 2 * u:2 * u + 2, :].rearrange("p c n -> p (c n)"), bank, IWS).then_inc(s["act_free"], 1)
                elif kind == "out":
                    for h in range(2):
                        square = 3072 + PW * (4 * i + 2 * u + h)
                        act.activation(Y[:, square:square + PW], bank[:, PW * h:PW * h + PW], ACT.Square, scale=IWS,
                                       accum_out=part[:, 2 * u + h, i:i + 1])
                    copy(Mseq[:, 2 * u:2 * u + 2, PW * i:PW * i + PW], bank.rearrange("p (h n) -> p h n", h=2), IWS)\
                        .then_inc(s["act_free"], 1)

            def before(p):
                if p > 0 and PANELS[p - 1][0] == "ga":
                    j = PANELS[p - 1][1]
                    act.wait_ge(s["lru_par"], 1)
                    for u in range(2):
                        t = 2 * j + u
                        act.wait_ge(s["lru_gates"], t + 1)
                        link(act.activation(rbuf[:, u, :], PS[:, 4 + 2 * u], ACT.Tanh, scale=0.5, bias=halfA[:, A_BR + t:A_BR + t + 1]))
                        act.activation(abuf[:, u, :], rbuf[:, u, :], ACT.Exp, scale=nsp4[:, t:t + 1], bias=nsp4[:, t:t + 1])\
                            .then_inc(s["lru_a"], 1)
                        act.activation(vbuf[:, u, :], rbuf[:, u, :], ACT.Tanh, scale=sp4[:, t:t + 1], bias=sp4[:, t:t + 1])\
                            .then_inc(s["lru_v"], 1)
                        act.activation(wbuf[:, u, :], PS[:, 5 + 2 * u], ACT.Tanh, scale=0.5, bias=halfA[:, A_BI + t:A_BI + t + 1])\
                            .then_inc(s["lru_w"], 1)
                    act.wait_ge(s["lru_vv"], 2 * j + 2)
                    act.activation(vbuf, vbuf, ACT.Sqrt).then_inc(s["lru_beta"], 1)
                    for u in range(2):
                        t = 2 * j + u
                        act.wait_ge(s["lru_y"], t + 1)
                        copy(Y_HI[0][:, t, :], hbuf[:, u, :]).then_inc(s["y_hi"], 1)
                if p > 0 and PANELS[p - 1][0] == "conv":
                    for u in range(2):
                        n = conv_tiles(p - 1) + u
                        act.wait_ge(s["conv_done"], n + 1)
                        if n - 8 >= 2:
                            act.wait_ge(s["conv_silu"], n - 8 - 1)
                        act.activation(rbuf[:, u, :], cbuf[:, u, :], ACT.Tanh, scale=0.5).then_inc(s["conv_tanh"], 1)
                if p in SSD_SLOT:
                    q = SSD_SLOT.index(p)
                    act.wait_ge(s["ssd_g"], q + 1)
                    if q > 0:
                        act.wait_ge(s["ssd_out"], q)
                    act.activation(est.rearrange("p j l -> p (j l)"), PS[:, 5:7, :].rearrange("p b n -> p (b n)"), ACT.Exp)\
                        .then_inc(s["ssd_exp"], 1)
                if p in SSD_END:
                    g = SSD_END[p]
                    act.wait_ge(s["ssd_y"], 4 * g + 4)
                    for c in range(ST):
                        link(act.activation(est.rearrange("p j l -> p (j l)")[:, 0:S], z[g][:, c, :], ACT.Square,
                                            accum_out=gss[:, c:c + 1]))
                    act.activation(gss, gss, ACT.Sqrt, scale=1.0 / (512 * P * P), bias=eps).then_inc(s["ssd_ss"], 1)
                if SWA0 <= p < SWA0 + 8:
                    for e in range(2):
                        n = 2 * (p - SWA0) + e
                        k0 = HD if n % 4 else P
                        act.wait_ge(s["sw_m"], n + 1)
                        if n >= 2:
                            act.wait_ge(s["sw_T"], n - 1)
                        for k in range(4):
                            act.activation(sE[:, e, k, k0:PW], PS[:, 4 + 2 * e + k // 2, PW * (k % 2) + k0:PW * (k % 2) + PW],
                                           ACT.Exp, bias=sm[:, e, k:k + 1], accum_out=ssum[:, e, k:k + 1])
                        act.activation(sd[:, e], sd[:, e], ACT.Exp).then_inc(s["sw_e"], 1)
                if DIFF0 <= p < DIFF0 + 16:
                    for e in range(2):
                        n = 2 * (p - DIFF0) + e
                        nk = (n % 4 + 1) * P
                        act.wait_ge(s["df_m"], n + 1)
                        act.activation(dE[:, e, 0, 0:nk], PS[:, 4 + 2 * e, 0:nk], ACT.Exp, bias=dm[:, e, 0:1], accum_out=dsum[:, e, 0:1])
                        link(act.activation(dE[:, e, 1, 0:nk], PS[:, 5 + 2 * e, 0:nk], ACT.Exp, bias=dm[:, e, 1:2],
                                            accum_out=dsum[:, e, 1:2]))
                        act.activation(dsum[:, e], dsum[:, e], ACT.Copy).then_inc(s["df_e"], 1)
                if p in DIFF_END:
                    act.wait_ge(s["df_ss"], DIFF_END[p] + 1)
                    act.activation(dss, dss, ACT.Sqrt, scale=1.0 / P, bias=eps).then_inc(s["df_sq"], 1)

            def between(p):
                if p == 0:
                    act.wait_ge(s["sp_in"], 1)
                    link(act.activation(ea, rowp[:, R_AL:R_AL + 16], ACT.Exp))
                    act.activation(spw[:, 2, :], spw[:, 1, :], ACT.Exp).then_inc(s["sp_exp"], 1)
                    act.wait_ge(s["lam_e"], 1)
                    act.activation(lsum, lsum, ACT.Exp).then_inc(s["lam_e"], 1)
                if p == 1:
                    act.wait_ge(s["cs_done"], 1)
                    act.wait_ge(s["cs_ready"], 1)
                    act.activation(ecs.rearrange("p c j -> p (c j)"), PS[:, 5, 0:64], ACT.Exp)
                    link(act.activation(cdec.rearrange("p c j -> p (c j)"), PS[:, 6, 0:64], ACT.Exp))
                    act.activation(dend.rearrange("p c j -> p (c j)"), dend.rearrange("p c j -> p (c j)"), ACT.Exp)\
                        .then_inc(s["dec_ready"], 1)
                if SWA0 <= p < SWA0 + 8:
                    for e in range(2):
                        n = 2 * (p - SWA0) + e
                        k0 = 0 if n % 4 else P
                        act.wait_ge(s["sw_T"], n + 1)
                        if n >= 2:
                            act.wait_ge(s["sw_o"], n - 1)
                        copy(sPT[:, e, 2:4, k0:PW], PS[:, 5 + 2 * e, :].rearrange("p (k n) -> p k n", k=2)[:, :, k0:PW])\
                            .then_inc(s["sw_Ta"], 1)
                if DIFF0 <= p < DIFF0 + 16:
                    for e in range(2):
                        n = 2 * (p - DIFF0) + e
                        nk = (n % 4 + 1) * P
                        act.wait_ge(s["df_T"], n + 1)
                        if n >= 2:
                            act.wait_ge(s["df_o"], n - 1)
                        copy(dPT[:, e, 0:nk], PS[:, 4 + 2 * e, 0:nk]).then_inc(s["df_Tr"], 1)

            def middle(p):
                if p > 0 and PANELS[p - 1][0] == "conv" and PANELS[p - 1][1] != 10:
                    i = PANELS[p - 1][1]
                    for u in range(2):
                        n = [8, 0, 2, 4, 6].index(i) * 2 + u
                        act.wait_ge(s["xt_done"], n + 1)
                        src = PS[:, 5 + 2 * u, :].rearrange("p (c n) -> p c n", c=ST)
                        if i == 8:
                            copy(Bseq[:, :, P * u:P * u + P], src).then_inc(s["xt_read"], 1)
                        else:
                            t = (i + u) % 4
                            copy(xs[i // 4][:, :, P * t:P * t + P], src, 0.5).then_inc(s["xt_read"], 1)
                if p in SSD_END:
                    g = SSD_END[p]
                    for t in range(4):
                        f = 4 * g + t
                        act.wait_ge(s["ssd_T"], f + 1)
                        copy(Y_HI[1][:, f, :], PS[:, 4 + t, :], colB[:, B_NG + f:B_NG + f + 1]).then_inc(s["yb_hi"], 1)
                if p in DIFF_END:
                    act.wait_ge(s["df_nT"], 2 * DIFF_END[p] + 2)
                if DIFF0 <= p < DIFF0 + 16:
                    for e in range(2):
                        n = 2 * (p - DIFF0) + e
                        act.wait_ge(s["df_o"], n + 1)
                        copy(dO[:, n % 8, :], PS[:, 5 + 2 * e, 0:P]).then_inc(s["df_or"], 1)
                if p > 0 and PANELS[p - 1][0] in ROTATED:
                    kind, i = PANELS[p - 1][0:2]
                    dst = {"kc": kC, "qc": qC[i % 2], "qd": qD[i % 2], "kd": kD[i % 2]}[kind]
                    if kind == "qc" and i >= 2:
                        act.wait_ge(s["sw_s"], 4 * (i - 1))
                    if kind in ("qd", "kd") and i >= 2:
                        act.wait_ge(s["df_s"], 8 * (i - 1))
                    if kind == "qc" and i == 0:
                        act.wait_ge(s["ssd_out"], 8)
                    act.wait_ge(s["rope_done"], rope_index(p - 1) + 1)
                    for t in range(2):
                        copy(dst[HD * t:HD * t + HD, t], rcos[HD * t:HD * t + HD]).then_inc(s["rope_hi"], 1)

            def after(p):
                if SWA0 <= p < SWA0 + 8:
                    for e in range(2):
                        n = 2 * (p - SWA0) + e
                        j, i = divmod(n, 4)
                        act.wait_ge(s["sw_y"], n + 1)
                        if n == 0:
                            act.wait_ge(s["tile_done"], 2 * (SLOT[("br", 3)] + 1))
                        copy(Y_HI[0][:, 2 * j:2 * j + 2, i * P:i * P + P], sy[:, e]).then_inc(s["y_hi"], 1)
                if p in DIFF_END:
                    h2 = DIFF_END[p]
                    for u in range(2):
                        act.wait_ge(s["df_y"], 2 * h2 + u + 1)
                        if h2 == 0 and u == 0:
                            act.wait_ge(s["tile_done"], 2 * (SLOT[("br", 7)] + 1))
                        copy(Y_HI[1][:, 2 * h2 + u, :], dy[:, u, :]).then_inc(s["y_hi"], 1)
                if PANELS[p][0] == "br" and PANELS[p][1] >= 12:
                    i = PANELS[p][1] - 12
                    for u in range(2):
                        act.wait_ge(s["m_acc"], 16 + 2 * i + u + 1)
                        if i == 0 and u == 0:
                            act.wait_ge(s["tile_done"], 2 * (SLOT[("br", 11)] + 1))
                        copy(Y_HI[0][:, 2 * i + u, :], M[:, 2 * i + u, :], 1.0 / P).then_inc(s["m_hi"], 1)

            act.activation(ss, nss, ACT.Sqrt, scale=1.0 / D, bias=eps).then_inc(s["ss_ready"], 1)
            act.wait_ge(s["cols_T"], 1)
            copy(colA[:, :], PS[:, 0, 0:A_N]).then_inc(s["cols_ready"], 1)
            copy(colB[:, :], PS[:, 1, 0:B_N]).then_inc(s["cols_ready"], 1)
            act.wait_ge(s["cols_ready"], 2)
            split_hi(0)
            for k in range(KT):
                act.wait_ge(s["xn_T"], k + 1)
                copy(hT[:, 0, k, :], PS[:, k, :], colA[:, A_G + k:A_G + k + 1]).then_inc(s["h_hi"], 1)
            copy(dtws[:, 0], dtw, WS).then_inc(s["dtw_hi"], 1)
            for p in range(NP):
                if p + 1 < NP:
                    split_hi(p + 1)
                before(p)
                evacuate(p, 0)
                between(p)
                middle(p)
                evacuate(p, 1)
                after(p)
            act.wait_ge(s["fin_sum"], 1)
            act.activation(ss, ss, ACT.Sqrt, scale=1.0 / D, bias=eps).then_inc(s["fin_ss"], 1)
            for n, q in enumerate((0, 2, 1, 3)):
                act.wait_ge(s["x_dve" if q >= 2 else "x_pool"], q % 2 + 1)
                act.activation(ys[:, 0, 1024 * n:1024 * n + 1024], xres[:, q, :], ACT.Square, accum_out=nss[:, q:q + 1])

        @block.vector
        def _(dve):
            chain = [0]

            def link(ins):
                chain[0] += 1
                ins.then_inc(s["dve_chain"], 1)
                dve.wait_ge(s["dve_chain"], chain[0])

            def stt(o, a, c, b, op0, op1):
                return dve.scalar_tensor_tensor(out=o, in0=a, scalar=c, in1=b, op0=op0, op1=op1)

            def tt(o, a, b, op):
                return dve.tensor_tensor(o, a, b, op)

            def split_lo(p):
                dve.wait_ge(s["hi_done"], p + 1)
                stt(wsp[:, p % NB, 1].rearrange("p k n -> p (k n)"), stage[:, p % NS].rearrange("p k n -> p (k n)"), WS,
                    wsp[:, p % NB, 0].rearrange("p k n -> p (k n)"), ALU.mult, ALU.subtract).then_inc(s["lo_done"], 1)

            def convolve(u, weights, col, step, bias):
                w = [weights[:, col + step * k:col + step * k + 1] for k in range(4)]
                link(dve.tensor_scalar(cbuf[:, u, :], xpad[:, u, 3:3 + S], w[3], bias, ALU.mult, ALU.add))
                for k in (2, 1):
                    link(stt(cbuf[:, u, :], xpad[:, u, k:k + S], w[k], cbuf[:, u, :], ALU.mult, ALU.add))
                stt(cbuf[:, u, :], xpad[:, u, 0:S], w[0], cbuf[:, u, :], ALU.mult, ALU.add).then_inc(s["conv_done"], 1)
                dve.wait_ge(s["conv_done"], conv_count[0] + 1)
                conv_count[0] += 1

            conv_count = [0]

            def evacuate(p, u):
                kind, i, _, _ = PANELS[p]
                tile = 2 * p + u
                bank = PS[:, tile % 4]
                if kind in ("ga", "z", "gc", "gd"):
                    dve.wait_ge(s["gate_ready"], gate_uses(tile))
                    if kind == "ga":
                        dst, g, b = gbuf[:, u, :], G[:, u], bank
                    elif kind == "z":
                        dst = z[i // 2][:, 2 * u:2 * u + 2, PW * (i % 2):PW * (i % 2) + PW]
                        g, b = G[:, u].rearrange("p (c n) -> p c n", c=2), bank.rearrange("p (c n) -> p c n", c=2)
                    else:
                        dst, g, b = (gC if kind == "gc" else gD)[i % 2][:, u, :], G[:, u], bank
                    stt(dst, g, 1.0, b, ALU.add, ALU.mult).then_inc(s["dve_free"], 1)
                elif kind in ("xa", "conv"):
                    dve.wait_ge(s["act_free"], act_frees(tile))
                    n = conv_tiles(p) + u - 8
                    if n >= 2:
                        dve.wait_ge(s["conv_silu"], n - 1)
                    if kind == "xa":
                        t = 2 * i + u
                        convolve(u, colA, A_CW + t, 8, colA[:, A_CB + t:A_CB + t + 1])
                    else:
                        t = i + u
                        convolve(u, colB, B_CW + t, 12, colB[:, B_CB + t:B_CB + t + 1])
                elif kind == "br":
                    dve.wait_ge(s["act_free"], act_frees(tile - 2))
                    dve.wait_ge(s["tile_done"], tile + 1)
                    if i < 4:
                        dst = M[:, 2 * i + u, :]
                    else:
                        n = 2 * (i - 4) + u
                        if n >= 2:
                            dve.wait_ge(s["m_acc"], n - 1)
                        dst = T[:, S * u:S * u + S]
                    stt(dst, G[:, u], 1.0, bank, ALU.add, ALU.mult).then_inc(s["dve_free"], 1)
                if u == 1 and kind in ROTATED:
                    dve.wait_ge(s["act_free"], act_frees(2 * p + 1))
                    n = rope_index(p)
                    if n >= 1:
                        dve.wait_ge(s["rope_hi"], 2 * n)
                        dve.wait_ge(s["rope_lo"], 2 * n)
                    link(tt(rcos, rraw, cosT.unsqueeze(1).to_broadcast([P, 2, S]), ALU.mult))

            def softplus():
                v, na, e, r, u, q, t, rl, sp_ = (spw[:, i, :] for i in range(9))
                link(dve.tensor_scalar(na, v, -1.0, None, ALU.mult))
                link(tt(na, na, v, ALU.min))
                dve.tensor_scalar(rl, v, 0.0, None, ALU.max).then_inc(s["sp_in"], 1)
                dve.wait_ge(s["sp_in"], 1)
                dve.wait_ge(s["sp_exp"], 1)
                link(dve.tensor_scalar(r, e, 2.0, None, ALU.add))
                link(dve.reciprocal(r, r))
                link(tt(u, e, r, ALU.mult))
                link(tt(q, u, u, ALU.mult))
                link(dve.tensor_scalar(t, q, 1.0 / 13, None, ALU.mult))
                for k in (11, 9, 7, 5, 3):
                    link(stt(t, t, 1.0 / k, q, ALU.add, ALU.mult))
                link(stt(t, t, 1.0, u, ALU.add, ALU.mult))
                link(stt(sp_, t, 2.0, rl, ALU.mult, ALU.add))
                return sp_

            def scores_in(p):
                if SWA0 <= p < SWA0 + 8:
                    for e in range(2):
                        n = 2 * (p - SWA0) + e
                        j = n // 4
                        k0 = HD if n % 4 else P
                        sink = rowp[:, R_SINK + 4 * j:R_SINK + 4 * j + 4].rearrange("p (s b) -> p b s", b=2)
                        m, d = (v[:, e].rearrange("p (b s) -> p b s", b=2) for v in (sm, sd))
                        dve.wait_ge(s["sw_s"], n + 1)
                        scores = PS[:, 4 + 2 * e:6 + 2 * e, :].rearrange("p b (s n) -> p b s n", s=2)[:, :, :, k0:PW]
                        link(dve.tensor_reduce(m, scores, AX, ALU.max))
                        link(tt(m, m, sink, ALU.max))
                        link(tt(d, sink, m, ALU.subtract))
                        dve.tensor_scalar(m, m, -1.0, None, ALU.mult).then_inc(s["sw_m"], 1)
                if DIFF0 <= p < DIFF0 + 16:
                    for e in range(2):
                        n = 2 * (p - DIFF0) + e
                        nk = (n % 4 + 1) * P
                        dve.wait_ge(s["df_s"], n + 1)
                        dve.tensor_reduce(dm[:, e], PS[:, 4 + 2 * e:6 + 2 * e, 0:nk], AX, ALU.max, negate=True).then_inc(s["df_m"], 1)
                if p in DIFF_END:
                    h2 = DIFF_END[p]
                    dve.wait_ge(s["df_or"], 8 * h2 + 8)
                    link(tt(dsq, dO, dO, ALU.mult))
                    dve.tensor_reduce(dss, dsq, AX, ALU.add).then_inc(s["df_ss"], 1)

            def before(p):
                if p > 0 and PANELS[p - 1][0] == "ga":
                    j = PANELS[p - 1][1]
                    for u in range(2):
                        t = 2 * j + u
                        dve.wait_ge(s["lru_a2"], t + 1)
                        stt(vbuf[:, u, :], rbuf[:, u, :], 1.0, vbuf[:, u, :], ALU.add, ALU.mult).then_inc(s["lru_vv"], 1)
                        dve.wait_ge(s["lru_w"], t + 1)
                        stt(wbuf[:, u, :], wbuf[:, u, :], 1.0, cbuf[:, u, :], ALU.add, ALU.mult).then_inc(s["lru_ww"], 1)
                    for u in range(2):
                        t = 2 * j + u
                        dve.wait_ge(s["lru_bw"], t + 1)
                        if t >= 2:
                            dve.wait_ge(s["y_lo"], t - 1)
                        link(dve.tensor_tensor_scan(hbuf[:, u, :], abuf[:, u, :], wbuf[:, u, :], 0.0, ALU.mult, ALU.add))
                        stt(hbuf[:, u, :], hbuf[:, u, :], 1.0 / 256, gbuf[:, u, :], ALU.mult, ALU.mult).then_inc(s["lru_y"], 1)
                if p > 0 and PANELS[p - 1][0] == "conv":
                    i = PANELS[p - 1][1]
                    for u in range(2):
                        n = conv_tiles(p - 1) + u - 8
                        dve.wait_ge(s["conv_tanh"], n + 1)
                        if i >= 8:
                            dst = (BT if i == 8 else CT)[:, u, :]
                            link(stt(dst, rbuf[:, u, :], 1.0, cbuf[:, u, :], ALU.add, ALU.mult))
                            dve.tensor_scalar(dst, dst, 0.5, None, ALU.mult).then_inc(s["conv_silu"], 1)
                        else:
                            if n >= 6:
                                dve.wait_ge(s["xt_done"], n - 3)
                            stt(wbuf[:, u, :], rbuf[:, u, :], 1.0, cbuf[:, u, :], ALU.add, ALU.mult).then_inc(s["conv_silu"], 1)
                if p in SSD_SLOT:
                    q = SSD_SLOT.index(p)
                    dve.wait_ge(s["ssd_g"], q + 1)
                    link(tt(gm, PS[:, 4, 0:P], tri, ALU.mult))
                    dve.wait_ge(s["ssd_exp"], q + 1)
                    tt(est, est, gm.unsqueeze(1).to_broadcast([P, 8, P]), ALU.mult).then_inc(s["ssd_mt"], 1)
                if p in SSD_END:
                    g = SSD_END[p]
                    dve.wait_ge(s["ssd_ss"], g + 1)
                    link(dve.reciprocal(grin, gss))
                    link(dve.tensor_scalar(grin, grin, 1.0 / P, None, ALU.mult))
                    tt(z[g], z[g], grin.unsqueeze(2).to_broadcast([P, ST, S]), ALU.mult).then_inc(s["ssd_norm"], 1)
                if SWA0 <= p < SWA0 + 8:
                    for e in range(2):
                        n = 2 * (p - SWA0) + e
                        k0 = HD if n % 4 else P
                        dve.wait_ge(s["sw_e"], n + 1)
                        link(tt(srin[:, e], ssum[:, e], sd[:, e], ALU.add))
                        link(dve.reciprocal(srin[:, e], srin[:, e]))
                        tt(sE[:, e, :, k0:PW], sE[:, e, :, k0:PW], srin[:, e].unsqueeze(2).to_broadcast([P, 4, PW - k0]), ALU.mult)\
                            .then_inc(s["sw_n"], 1)
                if DIFF0 <= p < DIFF0 + 16:
                    for e in range(2):
                        n = 2 * (p - DIFF0) + e
                        nk = (n % 4 + 1) * P
                        dve.wait_ge(s["df_e"], n + 1)
                        link(dve.reciprocal(drin[:, e], dsum[:, e]))
                        link(tt(drin[:, e, 1:2], drin[:, e, 1:2], nlam, ALU.mult))
                        if n >= 2:
                            dve.wait_ge(s["df_T"], n - 1)
                        link(dve.tensor_scalar(dA[:, e, 0:nk], dE[:, e, 0, 0:nk], drin[:, e, 0:1], None, ALU.mult))
                        stt(dA[:, e, 0:nk], dE[:, e, 1, 0:nk], drin[:, e, 1:2], dA[:, e, 0:nk], ALU.mult, ALU.add).then_inc(s["df_a"], 1)

            def between(p):
                if p in DIFF_END:
                    h2 = DIFF_END[p]
                    dve.wait_ge(s["df_sq"], h2 + 1)
                    link(dve.reciprocal(drs, dss))
                    tt(dO, dO, drs.unsqueeze(2).to_broadcast([P, 8, P]), ALU.mult).then_inc(s["df_n"], 1)
                if p == 0:
                    dve.wait_ge(s["dt_raw"], 1)
                    bias = rowp[:, R_DTB:R_DTB + 16].unsqueeze(1).to_broadcast([P, ST, 16])
                    link(stt(spw[:, 0, 0:64].rearrange("p (c j) -> p c j", c=ST), PS[:, 4, 0:64].rearrange("p (c j) -> p c j", c=ST),
                             IWS, bias, ALU.mult, ALU.add))
                    link(dve.tensor_scalar(spw[:, 0, 64:72], colA[:, A_LAM:A_LAM + 8], -1.0, None, ALU.mult))
                    sp_ = softplus()
                    link(dve.tensor_copy(dtv.rearrange("p c j -> p (c j)"), sp_[:, 0:64]))
                    stt(dta, dtv, -1.0, ea.unsqueeze(1).to_broadcast([P, ST, 16]), ALU.mult, ALU.mult).then_inc(s["dta_ready"], 1)
                    link(dve.tensor_scalar(sp4, sp_[:, 64:72], 4.0, None, ALU.mult))
                    dve.tensor_scalar(nsp4, sp_[:, 64:72], -4.0, None, ALU.mult).then_inc(s["lru_par"], 1)
                    prod = spw[:, 8:10, :].rearrange("p i n -> p (i n)")[:, 0:128].rearrange("p (i n) -> p i n", i=2)
                    lq = rowp[:, R_LQ:R_LQ + 256].rearrange("p (i t n) -> p i t n", i=2, t=2)
                    dve.wait_ge(s["dta_ready"], 1)
                    dve.wait_ge(s["lru_par"], 1)
                    link(tt(prod, lq[:, :, 0, :], lq[:, :, 1, :], ALU.mult))
                    dve.tensor_reduce(lsum, prod, AX, ALU.add).then_inc(s["lam_e"], 1)
                    dve.wait_ge(s["lam_e"], 2)
                    link(tt(nlam, lsum[:, 1:2], lsum[:, 0:1], ALU.subtract))
                    link(tt(nlam, nlam, rowp[:, R_LI:R_LI + 1], ALU.subtract))
                    link(stt(ng2, colB[:, B_DG:B_DG + 1], 1.0 / P, rowp[:, R_LI + 1:R_LI + 2], ALU.mult, ALU.mult))
                if p == 1:
                    dve.wait_ge(s["cs_done"], 1)
                    link(dve.tensor_copy(cs.rearrange("p c j -> p (c j)"), PS[:, 5, 0:64]))
                    tt(dend.rearrange("p c j -> p (c j)"), PS[:, 6, 0:64], cs.rearrange("p c j -> p (c j)"), ALU.subtract)\
                        .then_inc(s["cs_ready"], 1)
                    dve.wait_ge(s["cs_ready"], 1)
                    link(dve.tensor_copy(dta16[:, 0], dta))
                    tt(dta16[:, 1], dta, dta16[:, 0], ALU.subtract).then_inc(s["dta16_ready"], 1)
                if p in SSD_SLOT:
                    q = SSD_SLOT.index(p)
                    g, c = divmod(q, 4)
                    yf = yt.rearrange("p j n -> p (j n)")
                    dve.wait_ge(s["ssd_out"], q + 1)
                    if c == 0:
                        dve.tensor_copy(state.rearrange("p j n -> p (j n)"), PS[:, 5, :]).then_inc(s["ssd_st"], 1)
                    elif c < 3:
                        link(tt(state, state, cdec[:, c, 8 * g:8 * g + 8].unsqueeze(2).to_broadcast([P, 8, HD]), ALU.mult))
                        tt(state.rearrange("p j n -> p (j n)"), state.rearrange("p j n -> p (j n)"), PS[:, 5, :], ALU.add)\
                            .then_inc(s["ssd_st"], 1)
                    link(tt(yf, yf, PS[:, 4, :], ALU.add))
                    if c > 0:
                        link(tt(inter[:, :, :], PS[:, 6, :].rearrange("p (j n) -> p j n", j=8),
                                ecs[:, c, 8 * g:8 * g + 8].unsqueeze(2).to_broadcast([P, 8, HD]), ALU.mult))
                        link(tt(yf, yf, inter[:, :, :].rearrange("p j n -> p (j n)"), ALU.add))
                    tt(z[g][:, c, :], z[g][:, c, :], yf, ALU.mult).then_inc(s["ssd_y"], 1)
                if SWA0 <= p < SWA0 + 8:
                    for e in range(2):
                        n = 2 * (p - SWA0) + e
                        k0 = 0 if n % 4 else P
                        dve.wait_ge(s["sw_T"], n + 1)
                        if n >= 2:
                            dve.wait_ge(s["sw_o"], n - 1)
                        dve.tensor_copy(sPT[:, e, 0:2, k0:PW], PS[:, 4 + 2 * e, :].rearrange("p (k n) -> p k n", k=2)[:, :, k0:PW])\
                            .then_inc(s["sw_Tv"], 1)

            def middle(p):
                if p in SSD_END:
                    g = SSD_END[p]
                    for t in range(4):
                        f = 4 * g + t
                        dve.wait_ge(s["yb_hi"], f + 1)
                        stt(Y_LO[1][:, f, :], PS[:, 4 + t, :], colB[:, B_NG + f:B_NG + f + 1], Y_HI[1][:, f, :], ALU.mult, ALU.subtract)\
                            .then_inc(s["yb_lo"], 1)
                if SWA0 <= p < SWA0 + 8:
                    for e in range(2):
                        n = 2 * (p - SWA0) + e
                        j, i = divmod(n, 4)
                        dve.wait_ge(s["sw_o"], n + 1)
                        if n >= 2:
                            dve.wait_ge(s["y_lo"], 8 + n - 1)
                        stt(sy[:, e], PS[:, 4 + 2 * e, 0:PW].rearrange("p (u n) -> p u n", u=2), 1.0 / P,
                            gC[j % 2][:, :, i * P:i * P + P], ALU.mult, ALU.mult).then_inc(s["sw_y"], 1)
                if p in DIFF_END:
                    h2 = DIFF_END[p]
                    for u in range(2):
                        dve.wait_ge(s["df_nT"], 2 * h2 + u + 1)
                        if h2 > 0:
                            dve.wait_ge(s["y_lo"], 24 + 2 * h2 - 1 + u)
                        stt(dy[:, u, :], PS[:, 4 + 2 * u, :], ng2, gD[h2 % 2][:, u, :], ALU.mult, ALU.mult).then_inc(s["df_y"], 1)
                if p > 0 and PANELS[p - 1][0] in ROTATED:
                    n = rope_index(p - 1)
                    dve.wait_ge(s["rope_sin"], n + 1)
                    tt(rcos, rcos, rswap, ALU.add).then_inc(s["rope_done"], 1)

            def after(p):
                if PANELS[p][0] == "br" and PANELS[p][1] >= 12:
                    i = PANELS[p][1] - 12
                    for u in range(2):
                        dve.wait_ge(s["m_hi"], 2 * i + u + 1)
                        stt(Y_LO[0][:, 2 * i + u, :], M[:, 2 * i + u, :], 1.0 / P, Y_HI[0][:, 2 * i + u, :], ALU.mult, ALU.subtract)\
                            .then_inc(s["m_lo"], 1)

            dve.wait_ge(s["ss_ready"], 1)
            link(dve.reciprocal(rin, ss))
            for q in range(ST):
                dve.tensor_scalar(Mseq[:, q, :], xres[:, q, :], rin[:, q:q + 1], None, ALU.mult).then_inc(s["xn_ready"], 1)
            dve.wait_ge(s["cols_ready"], 2)
            link(dve.tensor_scalar(halfA[:, :], colA[:, :], 0.5, None, ALU.mult))
            split_lo(0)
            for k in range(KT):
                dve.wait_ge(s["h_hi"], k + 1)
                stt(hT[:, 1, k, :], PS[:, k, :], colA[:, A_G + k:A_G + k + 1], hT[:, 0, k, :], ALU.mult, ALU.subtract)\
                    .then_inc(s["h_lo"], 1)
            dve.wait_ge(s["dtw_hi"], 1)
            stt(dtws[:, 1].rearrange("p k n -> p (k n)"), dtw.rearrange("p k n -> p (k n)"), WS,
                dtws[:, 0].rearrange("p k n -> p (k n)"), ALU.mult, ALU.subtract).then_inc(s["dtw_lo"], 1)
            link(dve.memset(xpad[:, :, 0:3], 0.0))
            for p in range(NP):
                scores_in(p)
                attention = DIFF0 <= p < DIFF0 + 16 or SWA0 <= p < SWA0 + 8
                if p + 1 < NP and not attention:
                    split_lo(p + 1)
                before(p)
                if p + 1 < NP and attention:
                    split_lo(p + 1)
                evacuate(p, 0)
                between(p)
                middle(p)
                evacuate(p, 1)
                after(p)
            dve.wait_ge(s["act_free"], act_frees(2 * NP - 1))
            dve.tensor_reduce(ss, part, AX, ALU.add).then_inc(s["fin_sum"], 1)
            dve.wait_ge(s["fin_ss"], 1)
            dve.wait_ge(s["post_in"], 16)
            link(dve.reciprocal(rin, ss))
            for q in range(ST):
                stt(Mseq[:, q, :], Mseq[:, q, :], rin[:, q:q + 1], pg, ALU.mult, ALU.mult).then_inc(s["fin_y"], 1)
                if q >= 2:
                    dve.wait_ge(s["fin_y"], q + 1)
                    tt(xres[:, q, :], xres[:, q, :], Mseq[:, q, :], ALU.add).then_inc(s["x_dve"], 1)

        @block.gpsimd
        def _(pool):
            def tt(o, a, b, op):
                return pool.tensor_tensor(o, a, b, op)

            def rope(p):
                n = rope_index(p)
                pool.wait_ge(s["rope_dma"], 64 * (n + 1))
                tt(rswap, rswap, sinT.unsqueeze(1).to_broadcast([P, 2, S]), ALU.mult).then_inc(s["rope_sin"], 1)

            def triangle(q):
                g, c = divmod(q, 4)
                if q == 0:
                    pool.wait_ge(s["dta16_ready"], 1)
                    pool.wait_ge(s["lru_gates"], 8)
                else:
                    pool.wait_ge(s["ssd_g"], q)
                for part16 in range(2):
                    tt(dtri[:, part16], tri16.unsqueeze(1).to_broadcast([P, 8, P]),
                       dta16[:, part16, c, 8 * g:8 * g + 8].unsqueeze(2).to_broadcast([P, 8, P]), ALU.mult)\
                        .then_inc(s["ssd_tri"], 1)

            def rotated_lo(p):
                kind, i = PANELS[p][0:2]
                n = rope_index(p)
                pool.wait_ge(s["rope_hi"], 2 * n + 2)
                if kind in ("qc", "qd"):
                    pool.wait_ge(s["rope_stack"], stacked_after(n - 1))
                hi = {"kc": kC, "qc": qC[i % 2], "qd": qD[i % 2], "kd": kD[i % 2]}[kind]
                for t in range(2):
                    own = slice(HD * t, HD * t + HD)
                    dst = {"kc": kloC[own, t], "qc": rlo[own], "qd": rlo[own], "kd": kloD[i % 2][own]}[kind]
                    tt(dst, rcos[own], hi[own, t], ALU.subtract).then_inc(s["rope_lo"], 1)
                    pool.wait_ge(s["rope_lo"], 2 * n + 1 + t)

            pool.memset(wbd.rearrange("p t r n -> p (t r n)"), 0.0).then_inc(s["wbd_zero"], 1)
            for p in range(NP):
                if p > 0 and PANELS[p - 1][0] == "ga":
                    j = PANELS[p - 1][1]
                    for u in range(2):
                        t = 2 * j + u
                        pool.wait_ge(s["lru_a"], t + 1)
                        pool.wait_ge(s["lru_v"], t + 1)
                        tt(rbuf[:, u, :], abuf[:, u, :], abuf[:, u, :], ALU.mult).then_inc(s["lru_a2"], 1)
                    pool.wait_ge(s["lru_beta"], j + 1)
                    for u in range(2):
                        t = 2 * j + u
                        pool.wait_ge(s["lru_ww"], t + 1)
                        tt(wbuf[:, u, :], wbuf[:, u, :], vbuf[:, u, :], ALU.mult).then_inc(s["lru_bw"], 1)
                    for u in range(2):
                        t = 2 * j + u
                        pool.wait_ge(s["y_hi"], t + 1)
                        tt(Y_LO[0][:, t, :], hbuf[:, u, :], Y_HI[0][:, t, :], ALU.subtract).then_inc(s["y_lo"], 1)
                if p in SSD_SLOT:
                    q = SSD_SLOT.index(p)
                    g, c = divmod(q, 4)
                    if q > 0:
                        pool.wait_ge(s["ssd_out"], q)
                        pool.wait_ge(s["ssd_y"], q)
                    if c == 0:
                        pool.wait_ge(s["xt_read"], 6 + 4 * g)
                        pool.wait_ge(s["dec_ready"], 1)
                        pool.wait_ge(s["dta_ready"], 1)
                    xv = xs[g][:, c, :].rearrange("p (j n) -> p j n", j=8)

                    def head(v):
                        return v.unsqueeze(2).to_broadcast([P, 8, HD])
                    hs = slice(8 * g, 8 * g + 8)
                    tt(xdt, xv, head(dtv[:, c, hs]), ALU.mult).then_inc(s["pool_chain"], 1)
                    tt(yt, xv, head(rowp[:, R_D + 8 * g:R_D + 8 * g + 8]), ALU.mult)
                    pool.wait_ge(s["pool_chain"], q + 1)
                    tt(xw, xdt, head(dend[:, c, hs]), ALU.mult).then_inc(s["ssd_x"], 1)
                    if q < 7:
                        triangle(q + 1)
                if p + 1 == SSD_SLOT[0]:
                    triangle(0)
                if p > 0 and PANELS[p - 1][0] in ROTATED:
                    rope(p - 1)
                    rotated_lo(p - 1)
                if p == SWA0 - 1:
                    pool.wait_ge(s["ssd_T"], 8)
                    pool.memset(sE[:, :, :, 0:HD], 0.0).then_inc(s["sw_zero"], 1)
                if SWA0 <= p < SWA0 + 8:
                    for e in range(2):
                        n = 2 * (p - SWA0) + e
                        j, i = divmod(n, 4)
                        pool.wait_ge(s["y_hi"], 8 + n + 1)
                        tt(Y_LO[0][:, 2 * j:2 * j + 2, i * P:i * P + P], sy[:, e], Y_HI[0][:, 2 * j:2 * j + 2, i * P:i * P + P],
                           ALU.subtract).then_inc(s["y_lo"], 1)
                if p in DIFF_END:
                    h2 = DIFF_END[p]
                    for u in range(2):
                        pool.wait_ge(s["y_hi"], 24 + 2 * h2 + u + 1)
                        tt(Y_LO[1][:, 2 * h2 + u, :], dy[:, u, :], Y_HI[1][:, 2 * h2 + u, :], ALU.subtract).then_inc(s["y_lo"], 1)
                if PANELS[p][0] == "br" and PANELS[p][1] >= 4:
                    i = PANELS[p][1]
                    for u in range(2):
                        pool.wait_ge(s["dve_free"], dve_frees(2 * p + u))
                        t = 2 * (i % 4) + u
                        tt(M[:, t, :], M[:, t, :], T[:, S * u:S * u + S], ALU.add).then_inc(s["m_acc"], 1)
            for q in range(2):
                pool.wait_ge(s["fin_y"], q + 1)
                tt(xres[:, q, :], xres[:, q, :], Mseq[:, q, :], ALU.add).then_inc(s["x_pool"], 1)

        block_guard.__exit__(None, None, None)
        for n in names:
            nc.gpsimd.sem_clear(s[n])
        nc.all_engine_barrier()
        layer_loop.__exit__(None, None, None)

        with nc.Block() as block:
            @block.sync
            def _(sp):
                sp.dma_start(out.rearrange("b (s p) n -> p (b s) n", p=P), xres[:, :, :]).then_inc(s["stored"], 16)
                sp.wait_ge(s["stored"], 16)


def stacked_after(n):
    return 64 + 32 * n


def rope_index(p):
    return sum(PANELS[q][0] in ROTATED for q in range(p))


def shape_constants():
    k = np.zeros((P, K_N), np.float32)
    i = np.arange(P)
    k[:, K_ID:K_ID + P] = np.eye(P)
    k[:, K_TRI:K_TRI + P] = i[:, None] <= i[None, :]
    k[:, K_STRICT:K_STRICT + P] = i[:, None] > i[None, :]
    k[:, K_ONES:K_ONES + P] = 1
    inv = (1.0 / (np.float32(10000.0) ** (np.arange(0, HD, 2, dtype=np.float32) / HD))).astype(np.float32)
    ang = (np.arange(S, dtype=np.float32)[None, :] * inv[i % 32][:, None]).astype(np.float32)
    k[:, K_COS:K_COS + S] = np.cos(ang)
    k[:, K_SIN:K_SIN + S] = np.sin(ang) * np.where(i % HD < 32, -1, 1)[:, None]
    for b in (0, HD):
        k[b, K_ML:K_ML + HD] = 1
        k[b + 1, K_ML + HD:K_ML + P] = 1
        k[b, K_MR:K_MR + HD] = NEG
        k[b, K_MR + 192:K_MR + 256] = NEG
        k[b + 1, K_MR:K_MR + P] = NEG
    return k


def kernel(**inputs):
    import concourse.bacc as bacc
    from concourse.bass_utils import run_bass_kernel_spmd

    a = {n: np.ascontiguousarray(v) for n, v in inputs.items()}
    tiles = lambda v: v.reshape(L, -1, P)
    li = np.array([[0.8 - 0.6 * math.exp(-0.3 * l)] for l in range(L)])
    arrays = {
        "x": a["x"], "w_in": a["w_in"], "w_branch": a["w_branch"].reshape(L * 4, D, D), "w_out": a["w_out"],
        "w_r": a["lru_w_r"], "w_i": a["lru_w_i"],
        "cols_a": np.concatenate([tiles(a[n]) for n in ("pre_norm_g", "b_merge", "lru_conv_w", "lru_conv_b", "lru_b_r",
                                                         "lru_b_i", "lru_lambda")], axis=1),
        "cols_b": np.concatenate([tiles(a[n]) for n in ("ssd_conv_w", "ssd_conv_b", "ssd_norm_g", "diff_norm_g")], axis=1),
        "rows": np.concatenate([a[n] for n in ("ssd_dt_bias", "ssd_a_log", "ssd_d", "swa_sinks", "diff_lq1", "diff_lk1",
                                               "diff_lq2", "diff_lk2")]
                               + [li.astype(np.float32), (1 - li).astype(np.float32)], axis=1).reshape(L, 1, R_N),
        "post_g": a["post_norm_g"].reshape(L, 1, D),
        "consts": shape_constants(),
    }
    nc = bacc.Bacc("TRN2", target_bir_lowering=False, num_devices=1)
    aps = [nc.dram_tensor(n, v.shape, F32, kind="ExternalInput").ap() for n, v in arrays.items()]
    res = nc.dram_tensor("out", (1, S, D), F32, kind="ExternalOutput").ap()
    program(nc, *aps, res)
    r = run_bass_kernel_spmd(nc, [arrays], core_ids=[0])
    return r.results[0]["out"]
```
